# Optimizing a Trainium2 kernel written in Bass

```python
import jax, jax.numpy as jnp
from jax import lax
import numpy as np

D_MODEL = 1024
BATCH = 1
SEQ = 2048
DEPTH = 1

GRID_W = 64
CTX_LEN = 256
D_MIX = D_MODEL
NDIR = 2
A_HEADS = 4
A_DK = 128
A_DV = 128
B_HEADS = 4
B_DK = 64
B_DV = 128
GLA_RANK = 16
GLA_NORMALIZER = 16.0
CONV_K = 3
DELTA_CHUNK = 64
GLA_CHUNK = 16
D_FF = -(-8 * D_MODEL // (3 * 256)) * 256
EPS = 1e-6
IN_SIZES = (A_HEADS * A_DK, A_HEADS * A_DK, A_HEADS * A_DV, A_HEADS * A_DV, NDIR * A_HEADS, NDIR * A_HEADS,
            B_HEADS * B_DK, B_HEADS * B_DK, B_HEADS * B_DV, B_HEADS * B_DV, NDIR * GLA_RANK)
IN_COLS = sum(IN_SIZES)

kernel_name = "hybrid_gdn_gla_prefix_block"

def rmsnorm(x, w):
    xf = x.astype(jnp.float32)
    y = xf * lax.rsqrt(jnp.mean(xf * xf, axis=-1, keepdims=True) + EPS) * w.astype(jnp.float32)
    return y.astype(x.dtype)

def modulate(h, shift, scale):
    return h * (1.0 + scale) + shift

def l2norm(t):
    return t * lax.rsqrt(jnp.sum(t * t, axis=-1, keepdims=True) + EPS)

def to_heads(t, n_heads):
    b, l, _ = t.shape
    return t.reshape(b, l, n_heads, -1).transpose(0, 2, 1, 3)

def from_heads(t):
    b, h, l, d = t.shape
    return t.transpose(0, 2, 1, 3).reshape(b, l, h * d)

def centred_conv_rows(u, w, n_rows):
    b, l, ch = u.shape
    row_len = l // n_rows
    pad = CONV_K // 2
    u = u.reshape(b, n_rows, row_len, ch)
    up = jnp.pad(u, ((0, 0), (0, 0), (pad, pad), (0, 0)))
    out = sum(w[tap] * up[:, :, tap:tap + row_len, :] for tap in range(CONV_K))
    return out.reshape(b, l, ch)

def gated_delta_chunked(q, k, v, beta, g, state0):
    bsz, h, l, dk = q.shape
    dv = v.shape[-1]
    c = DELTA_CHUNK
    n = l // c
    q = q.reshape(bsz, h, n, c, dk)
    k = k.reshape(bsz, h, n, c, dk)
    v = v.reshape(bsz, h, n, c, dv)
    beta = beta.reshape(bsz, h, n, c)
    gc = jnp.cumsum(g.reshape(bsz, h, n, c), axis=-1)
    idx = jnp.arange(c)
    incl = idx[:, None] >= idx[None, :]
    strict = idx[:, None] > idx[None, :]
    decay = jnp.exp(jnp.where(incl, gc[..., :, None] - gc[..., None, :], -jnp.inf))
    kb = k * beta[..., None]
    lower = jnp.where(strict, jnp.einsum('bhnid,bhnjd->bhnij', kb, k) * decay, 0.0)
    system = lower + jnp.eye(c, dtype=q.dtype)
    rhs = jnp.concatenate([v * beta[..., None], kb * jnp.exp(gc)[..., None]], axis=-1)
    sol = lax.linalg.triangular_solve(system, rhs, left_side=True, lower=True)
    u, w = sol[..., :dv], sol[..., dv:]
    qk = jnp.einsum('bhnid,bhnjd->bhnij', q, k) * decay
    q_dec = q * jnp.exp(gc)[..., None]
    k_dec = k * jnp.exp(gc[..., -1:] - gc)[..., None]
    g_last = jnp.exp(gc[..., -1])

    def step(s, xs):
        u_n, w_n, qd_n, kd_n, qk_n, gl_n = xs
        v_new = u_n - jnp.einsum('bhck,bhkv->bhcv', w_n, s)
        o_n = jnp.einsum('bhck,bhkv->bhcv', qd_n, s) + jnp.einsum('bhij,bhjv->bhiv', qk_n, v_new)
        s = s * gl_n[..., None, None] + jnp.einsum('bhck,bhcv->bhkv', kd_n, v_new)
        return s, o_n

    xs = tuple(jnp.moveaxis(t, 2, 0) for t in (u, w, q_dec, k_dec, qk, g_last))
    s_final, o = lax.scan(step, state0, xs)
    return jnp.moveaxis(o, 0, 2).reshape(bsz, h, l, dv), s_final

def gla_chunked(q, k, v, gk, state0):
    bsz, h, l, dk = q.shape
    dv = v.shape[-1]
    c = GLA_CHUNK
    n = l // c
    q = q.reshape(bsz, h, n, c, dk)
    k = k.reshape(bsz, h, n, c, dk)
    v = v.reshape(bsz, h, n, c, dv)
    bc = jnp.cumsum(gk.reshape(bsz, h, n, c, dk), axis=-2)
    idx = jnp.arange(c)
    incl = (idx[:, None] >= idx[None, :])[:, :, None]
    rel = jnp.exp(jnp.where(incl, bc[..., :, None, :] - bc[..., None, :, :], -jnp.inf))
    scores = jnp.sum(q[..., :, None, :] * k[..., None, :, :] * rel, axis=-1)
    o_intra = jnp.einsum('bhnij,bhnjv->bhniv', scores, v)
    q_dec = q * jnp.exp(bc)
    k_dec = k * jnp.exp(bc[..., -1:, :] - bc)
    g_last = jnp.exp(bc[..., -1, :])

    def step(s, xs):
        qd_n, kd_n, v_n, gl_n = xs
        o_n = jnp.einsum('bhck,bhkv->bhcv', qd_n, s)
        s = s * gl_n[..., None] + jnp.einsum('bhck,bhcv->bhkv', kd_n, v_n)
        return s, o_n

    xs = tuple(jnp.moveaxis(t, 2, 0) for t in (q_dec, k_dec, v, g_last))
    s_final, o_inter = lax.scan(step, state0, xs)
    o = jnp.moveaxis(o_inter, 0, 2) + o_intra
    return o.reshape(bsz, h, l, dv), s_final

def bidirectional_scan(scan_fn, ctx_dirs, lat_dirs, state0):
    o_ctx, o_lat = 0.0, 0.0
    for d in range(NDIR):
        c_in, x_in = ctx_dirs[d], lat_dirs[d]
        if d == 1:
            c_in = tuple(jnp.flip(t, axis=2) for t in c_in)
            x_in = tuple(jnp.flip(t, axis=2) for t in x_in)
        oc, s_ctx = scan_fn(*c_in, state0)
        ox, _ = scan_fn(*x_in, s_ctx)
        if d == 1:
            oc, ox = jnp.flip(oc, axis=2), jnp.flip(ox, axis=2)
        o_ctx = o_ctx + oc
        o_lat = o_lat + ox
    return o_ctx, o_lat

def project_side(h, n_rows, w_in, conv_w, a_log, dt_bias, gla_w2, gla_b):
    bsz, l, _ = h.shape
    p = (h @ w_in).astype(jnp.float32)
    points = [int(s) for s in np.cumsum(IN_SIZES)[:-1]]
    aq, ak, av, az, abeta, aa, bq, bk, bv, bg, blr = jnp.split(p, points, axis=-1)
    qkv = jax.nn.silu(centred_conv_rows(jnp.concatenate([aq, ak, av], axis=-1), conv_w.astype(jnp.float32), n_rows))
    aq, ak, av = jnp.split(qkv, 3, axis=-1)
    beta = jax.nn.sigmoid(abeta).reshape(bsz, l, NDIR, A_HEADS).transpose(2, 0, 3, 1)
    g = -jnp.exp(a_log.astype(jnp.float32)) * jax.nn.softplus(aa.reshape(bsz, l, NDIR, A_HEADS) + dt_bias.astype(jnp.float32))
    g = g.transpose(2, 0, 3, 1)
    gk = jnp.einsum('blnr,nrk->nblk', blr.reshape(bsz, l, NDIR, GLA_RANK), gla_w2.astype(jnp.float32))
    gk = jax.nn.log_sigmoid(gk + gla_b.astype(jnp.float32)[:, None, None, :]) / GLA_NORMALIZER
    gk = gk.reshape(NDIR, bsz, l, B_HEADS, B_DK).transpose(0, 1, 3, 2, 4)
    return {
        'a_q': l2norm(to_heads(aq, A_HEADS)) * A_DK ** -0.5,
        'a_k': l2norm(to_heads(ak, A_HEADS)),
        'a_v': to_heads(av, A_HEADS),
        'a_beta': beta, 'a_g': g, 'a_z': az,
        'b_q': to_heads(bq, B_HEADS) * B_DK ** -0.5,
        'b_k': to_heads(bk, B_HEADS),
        'b_v': to_heads(bv, B_HEADS),
        'b_gk': gk, 'b_g': bg,
    }

def gated_head_norm(o, w, z, n_heads):
    on = o * lax.rsqrt(jnp.mean(o * o, axis=-1, keepdims=True) + EPS) * w.astype(jnp.float32)
    return from_heads(on * jax.nn.silu(to_heads(z, n_heads)))

def token_mixers(h_x, h_c, n_rows, w_in, conv_w, a_log, dt_bias, gdn_norm, gla_w2, gla_b, gla_norm):
    sx = project_side(h_x, n_rows, w_in, conv_w, a_log, dt_bias, gla_w2, gla_b)
    sc = project_side(h_c, 1, w_in, conv_w, a_log, dt_bias, gla_w2, gla_b)
    bsz = h_x.shape[0]
    zero_a = jnp.zeros((bsz, A_HEADS, A_DK, A_DV), jnp.float32)
    zero_b = jnp.zeros((bsz, B_HEADS, B_DK, B_DV), jnp.float32)
    gdn_c, gdn_x = bidirectional_scan(
        gated_delta_chunked,
        [(sc['a_q'], sc['a_k'], sc['a_v'], sc['a_beta'][d], sc['a_g'][d]) for d in range(NDIR)],
        [(sx['a_q'], sx['a_k'], sx['a_v'], sx['a_beta'][d], sx['a_g'][d]) for d in range(NDIR)],
        zero_a)
    gla_c, gla_x = bidirectional_scan(
        gla_chunked,
        [(sc['b_q'], sc['b_k'], sc['b_v'], sc['b_gk'][d]) for d in range(NDIR)],
        [(sx['b_q'], sx['b_k'], sx['b_v'], sx['b_gk'][d]) for d in range(NDIR)],
        zero_b)
    mix_x = jnp.concatenate([gated_head_norm(gdn_x, gdn_norm, sx['a_z'], A_HEADS),
                             gated_head_norm(gla_x, gla_norm, sx['b_g'], B_HEADS)], axis=-1)
    mix_c = jnp.concatenate([gated_head_norm(gdn_c, gdn_norm, sc['a_z'], A_HEADS),
                             gated_head_norm(gla_c, gla_norm, sc['b_g'], B_HEADS)], axis=-1)
    return mix_x.astype(h_x.dtype), mix_c.astype(h_c.dtype)

def swiglu(h, w_gate, w_up, w_down):
    return (jax.nn.silu(h @ w_gate) * (h @ w_up)) @ w_down

def setup_inputs(seed: int = 0) -> dict:
    key = jax.random.key(seed)
    ks = jax.random.split(key, 24)
    f32 = jnp.float32
    nrm = lambda k, shape, scale: jax.random.normal(k, shape, f32) * scale
    gain = lambda k, shape: 1.0 + 0.02 * jax.random.normal(k, shape, f32)
    dt = jnp.exp(jax.random.uniform(ks[9], (DEPTH, NDIR, A_HEADS), f32, np.log(0.001), np.log(0.1)))
    return {
        'x': nrm(ks[0], (BATCH, SEQ, D_MODEL), 1.0),
        'c': nrm(ks[1], (BATCH, D_MODEL), 1.0),
        'ctx': nrm(ks[2], (BATCH, CTX_LEN, D_MODEL), 1.0),
        'c_ctx': nrm(ks[3], (D_MODEL,), 1.0),
        'w_mod': nrm(ks[4], (DEPTH, D_MODEL, 6 * D_MODEL), D_MODEL ** -0.5),
        'b_mod': nrm(ks[5], (DEPTH, 6 * D_MODEL), 0.02),
        'attn_norm': gain(ks[6], (DEPTH, D_MODEL)),
        'w_in': nrm(ks[7], (DEPTH, D_MODEL, IN_COLS), D_MODEL ** -0.5),
        'conv_w': nrm(ks[8], (DEPTH, CONV_K, 3 * A_HEADS * A_DK), CONV_K ** -0.5),
        'a_log': jnp.log(jax.random.uniform(ks[10], (DEPTH, NDIR, A_HEADS), f32, 1.0, 16.0)),
        'dt_bias': dt + jnp.log(-jnp.expm1(-dt)),
        'gdn_norm': gain(ks[11], (DEPTH, A_DV)),
        'gla_w2': nrm(ks[12], (DEPTH, NDIR, GLA_RANK, B_HEADS * B_DK), GLA_RANK ** -0.5),
        'gla_b': nrm(ks[13], (DEPTH, NDIR, B_HEADS * B_DK), 0.1),
        'gla_norm': gain(ks[14], (DEPTH, B_DV)),
        'w_out': nrm(ks[15], (DEPTH, D_MIX, D_MODEL), D_MIX ** -0.5),
        'ffn_norm': gain(ks[16], (DEPTH, D_MODEL)),
        'w_gate': nrm(ks[17], (DEPTH, D_MODEL, D_FF), D_MODEL ** -0.5),
        'w_up': nrm(ks[18], (DEPTH, D_MODEL, D_FF), D_MODEL ** -0.5),
        'w_down': nrm(ks[19], (DEPTH, D_FF, D_MODEL), D_FF ** -0.5),
        'final_norm': gain(ks[20], (D_MODEL,)),
    }

def reference(x, c, ctx, c_ctx, w_mod, b_mod, attn_norm, w_in, conv_w, a_log, dt_bias, gdn_norm,
              gla_w2, gla_b, gla_norm, w_out, ffn_norm, w_gate, w_up, w_down, final_norm):
    n_rows = x.shape[1] // GRID_W
    silu_c = jax.nn.silu(c)
    silu_cc = jax.nn.silu(c_ctx)
    for layer in range(DEPTH):
        mod_x = (silu_c @ w_mod[layer] + b_mod[layer])[:, None, :]
        mod_c = silu_cc @ w_mod[layer] + b_mod[layer]
        sh1, sc1, g1, sh2, sc2, g2 = jnp.split(mod_x, 6, axis=-1)
        csh1, csc1, cg1, csh2, csc2, cg2 = jnp.split(mod_c, 6, axis=-1)
        h_x = modulate(rmsnorm(x, attn_norm[layer]), sh1, sc1)
        h_c = modulate(rmsnorm(ctx, attn_norm[layer]), csh1, csc1)
        mix_x, mix_c = token_mixers(h_x, h_c, n_rows, w_in[layer], conv_w[layer], a_log[layer], dt_bias[layer],
                                    gdn_norm[layer], gla_w2[layer], gla_b[layer], gla_norm[layer])
        x = x + g1 * (mix_x @ w_out[layer])
        x = x + g2 * swiglu(modulate(rmsnorm(x, ffn_norm[layer]), sh2, sc2), w_gate[layer], w_up[layer], w_down[layer])
        if layer + 1 < DEPTH:
            ctx = ctx + cg1 * (mix_c @ w_out[layer])
            ctx = ctx + cg2 * swiglu(modulate(rmsnorm(ctx, ffn_norm[layer]), csh2, csc2), w_gate[layer], w_up[layer], w_down[layer])
    return rmsnorm(x, final_norm)


_drawn_inputs = setup_inputs


def setup_inputs(seed=0):
    import zlib

    import numpy as np

    out = dict(_drawn_inputs(seed))
    spreads = {}
    factors = {'ctx': 3.352,
     'attn_norm': 3.566,
     'gdn_norm': 22.482,
     'gla_b': 2.719,
     'gla_norm': 25.265,
     'ffn_norm': 13.362,
     'final_norm': 8.581}
    for name, (base, spread) in spreads.items():
        noise = np.random.default_rng([zlib.crc32(name.encode()), seed]).standard_normal(out[name].shape)
        drawn = base * np.exp(spread * noise) if base else spread * noise
        out[name] = __import__('jax').numpy.asarray(drawn.astype(out[name].dtype))
    for name, factor in factors.items():
        out[name] = (out[name] * factor).astype(out[name].dtype)
    return out
```

```python
from contextlib import ExitStack

import numpy as np

import concourse.bass as bass
from concourse import mybir

F32 = mybir.dt.float32
I8 = mybir.dt.int8
ACT = mybir.ActivationFunctionType
ALU = mybir.AluOpType
AX = mybir.AxisListType

P = 128
D = 1024
KD = D // P
SEQ, CTX = 2048, 256
EPS = 1e-6
HA = 4
DFF = 2816
FC = DFF // P
IN_COLS = 3632
GRID_W = 64
CONV_K = 3
NORMALIZER = 16.0
CHUNKS_CTX, CHUNKS = CTX // P, (CTX + SEQ) // P
W_Q, W_K, W_V, W_Z, W_BETA, W_BQ, W_BK, W_BV, W_BG, W_LR = 0, 512, 1024, 1536, 2048, 2064, 2320, 2576, 3088, 3600

R_KQ = 0
R_BQ = R_KQ + 2 * HA * P
R_BK = R_BQ + 2 * P
R_KTOK = R_BK + 2 * P
R_V = R_KTOK + 512
R_BV = R_V + 512
R_BKTOK = R_BV + 512
R_NB = R_BKTOK + 256
R_G = R_NB + 8
R_GK = R_G + 8
MIX = R_GK + 512
R_Z = MIX
R_BG = R_Z + 512
REC = R_BG + 512

SIZES = [1, 2, 4, 8, 16, 32, 64]
BLOCKS = [64, 32, 16]
NLEV = len(SIZES) - 1

C_ID, C_ONE, C_TRI, C_SUF, C_NEG, C_W = 0, 1, 2, 4, 6, 8
NTAB = C_W + 2 * (len(BLOCKS) + 2)
M_LEV, M_FIRST_T, M_BLK = 0, len(SIZES), len(SIZES) + 1
NMASK = M_BLK + len(BLOCKS) + 1


def tables():
    t = np.arange(P)
    a, b = t[:, None], t[None, :]
    tri = (a <= b).astype(np.float32)
    suf = (a > b).astype(np.float32)
    neg = np.where(b >= a, 0.0, -1e30).astype(np.float32)
    w = [tri]
    blk = []
    for s in BLOCKS:
        r = b // (2 * s) * 2 * s + s - 1
        w.append(np.where(b > r, (a > r) & (a <= b), (a > b) & (a <= r)).astype(np.float32))
        blk.append((a // (2 * s) == b // (2 * s)) & (b // s % 2 == 1) & (a // s % 2 == 0))
    s = BLOCKS[-1]
    m = b // s * s + s // 2 - 1
    w.append(((a > m) & (a <= b)).astype(np.float32) - ((a > b) & (a <= m)).astype(np.float32))
    blk.append((a // s == b // s) & (b >= a))
    lev = [(a // (2 * s) == b // (2 * s)) & (a // s % 2 == 1) & (b // s % 2 == 0) for s in SIZES]
    masks = [x.astype(np.float32) for x in [*lev, lev[0].T, *blk]]
    both = lambda x: [x, x[::-1, ::-1]]
    cols = [np.eye(P, dtype=np.float32), np.ones((P, P), np.float32), *both(tri), *both(suf), *both(neg)]
    cols += [x for x in w] + [x[::-1, ::-1] for x in w]
    mcols = [x for x in masks] + [x[::-1, ::-1] for x in masks]
    return (np.ascontiguousarray(np.concatenate(cols, 1), dtype=np.float32),
            np.ascontiguousarray(np.concatenate(mcols, 1), dtype=np.float32))


def wait(eng, sem, value):
    if not (isinstance(value, int) and value <= 0):
        eng.wait_ge(sem, value)


def semaphores(nc):
    made = []

    def sem(name):
        made.append(nc.alloc_semaphore(name))
        return made[-1]

    def clear():
        nc.clear_and_free_semaphores(made)
        nc.all_engine_barrier()

    return sem, clear


def rows(ap, n):
    return ap.unsqueeze(1).broadcast_to([ap.shape[0], n, ap.shape[1]])


def lanes(ap, n):
    return ap.unsqueeze(2).broadcast_to([ap.shape[0], ap.shape[1], n])


TB = 2
BT = TB * P
NBLK = (CTX + SEQ) // BT
T_COLS = [W_Q, W_Q + 256, W_K, W_K + 256, W_V, W_V + 256, W_BQ, W_BK]
TOK_JOBS = {8: (0, W_Z, R_Z), 9: (0, W_BG, R_BG), 12: (0, W_BV, R_BV),
            13: (1, W_Z, R_Z), 14: (1, W_BG, R_BG), 15: (1, W_BV, R_BV)}
TURNS = ["V0", "V1", "H0", "H1", "H2", "H3", "BK", "K0", "K1", "LR", "G0", "G1"]
BY_ACT = ["V0", "H0", "H2", "BK", "K1"]
BY_DVE = ["V1", "H1", "H3", "K0", "LR", "G0", "G1"]
NT, NTA, NTV = len(TURNS), len(BY_ACT), len(BY_DVE)


def stage_project(nc, t, rec, col, silu_c):
    with ExitStack() as ctx:
        sb = lambda name, shape, dt=F32: ctx.enter_context(nc.sbuf_tensor(name, shape, dt))
        bank = lambda name: ctx.enter_context(nc.psum_tensor(name, [P, 512], F32))
        sem, clear = semaphores(nc)
        ctx.callback(clear)
        tab = sb("tab", [P, 2, P])
        ident, ones = tab[:, 0, :], tab[:, 1, :]
        win = sb("win", [P, KD, IN_COLS])
        recb = sb("recb", [P, TB, REC])
        wst = recb[:, :, 0:KD * 512 // 1].rearrange("p t (k n) -> p t k n", k=KD)
        ytmp = sb("ytmp", [P, 12, BT])
        sq = sb("sq", [P, 2, 512])
        rs = sb("rs", [P, 2, 512])
        xt = sb("xt", [P, TB, D])
        hT = sb("hT", [P, 2, KD, BT])
        rowt = sb("rowt", [116, P])
        mod = sb("mod", [P, 2 * KD, 2])
        gain = sb("gain", [P, 2, KD])
        ss = sb("ss", [P, TB])
        rstd = sb("rstd", [P, TB])
        small = sb("small", [P, TB, 48])
        gate = sb("gate", [P, 3, TB, 8])
        dtb = sb("dtb", [P, 8])
        nega = sb("nega", [P, 8])
        eps = sb("eps", [P, 1])
        blrT = sb("blrT", [33, BT])
        w2 = sb("w2", [33, 512])
        PA = [bank(f"acc{i}") for i in range(4)]
        PT = [bank(f"turn{i}") for i in range(2)]
        PL = [bank(f"norm{i}") for i in range(2)]

        tab_in, rows_in, heads_in, small_in, w_in_in = sem("tab_in"), sem("rows_in"), sem("heads_in"), sem("small_in"), sem("w_in_in")
        wmod_in = [sem(f"wmod_in{i}") for i in range(2)]
        x_in, rec_out = sem("x_in"), sem("rec_out")
        cols_full, cols_done, zeroed = sem("cols_full"), sem("cols_done"), sem("zeroed")
        silu_a, silu_v, mod_full, mod_done, nega_a, nega_done = (
            sem("silu_a"), sem("silu_v"), sem("mod_full"), sem("mod_done"), sem("nega_a"), sem("nega_done"))
        job_full, conv_step, conv_done, silu_done = sem("job_full"), sem("conv_step"), sem("conv_done"), sem("silu_done")
        act_evac, narrow_done = sem("act_evac"), sem("narrow_done")
        sq_done, l2_full, l2_ln, rs_done, qk_done = sem("sq_done"), sem("l2_full"), sem("l2_ln"), sem("rs_done"), sem("qk_done")
        turn_full, turn_act, turn_dve = sem("turn_full"), sem("turn_act"), sem("turn_dve")
        ss_done, rstd_ln, rstd_done, xs_done = sem("ss_done"), sem("rstd_ln"), sem("rstd_done"), sem("xs_done")
        gate_a, gate_v, gk_a, gk_ln = sem("gate_a"), sem("gate_v"), sem("gk_a"), sem("gk_ln")
        block = ctx.enter_context(nc.Block())

        x_v = t["x"].rearrange("o (b t p) d -> (o b) p t d", t=TB, p=P)
        c_v = t["ctx"].rearrange("o (t p) d -> (o p) t d", p=P)
        rec_v = rec.rearrange("(b t) p n -> b p t n", t=TB)
        wmod_v = t["w_mod"].rearrange("o (k p) n -> (o p) k n", p=P)
        win_v = t["w_in"].rearrange("o (k p) n -> (o p) k n", p=P)

        def names(last):
            return [n for n in TURNS if not (last and n[0] == "H")]

        def turn_at(b, name, last=False):
            return PT[TURNS.index(name) % 2], 4 + b * NT + names(last).index(name) + 1

        def turn_gone(eng, b, name, last=False):
            act_names = [n for n in names(last) if n in BY_ACT]
            if name in BY_ACT:
                wait(eng, turn_act, 2 + b * NTA + act_names.index(name) + 1)
            else:
                dve_names = [n for n in names(last) if n in BY_DVE]
                wait(eng, turn_dve, 2 + b * NTV + dve_names.index(name) + 1)

        def turn_free(eng, b, name, last=False):
            i = names(last).index(name)
            if i >= 2:
                turn_gone(eng, b, names(last)[i - 2], last)
            elif isinstance(b, int) and b == 0:
                wait(eng, turn_dve if i else turn_act, 2)
            else:
                turn_gone(eng, b - 1, TURNS[NT - 2 + i])

        def job_gone(eng, b, j):
            if j < 6:
                wait(eng, conv_done, b * 6 + j + 1)
            elif j in (10, 11):
                wait(eng, narrow_done, b * 2 + j - 9)
            else:
                wait(eng, act_evac, b * 8 + (j - 5 if j < 10 else j - 7))

        @block.sync
        def _(sp):
            sp.dma_start(tab[:, :, :], t["table"][:, 0:2 * P].rearrange("p (a b) -> p a b", a=2)).then_inc(tab_in, 16)
            sp.dma_start(rowt[0:48, :], t["b_mod"].rearrange("o (r p) -> (o r) p", p=P)).then_inc(rows_in, 16)
            sp.dma_start(rowt[48:56, :], t["attn_norm"].rearrange("o (r p) -> (o r) p", p=P)).then_inc(rows_in, 16)
            sp.dma_start(rowt[56:64, :], t["ffn_norm"].rearrange("o (r p) -> (o r) p", p=P)).then_inc(rows_in, 16)
            sp.dma_start(rowt[64:72, :], t["c"].rearrange("o (r p) -> (o r) p", p=P)).then_inc(rows_in, 16)
            sp.dma_start(rowt[72:80, :], t["c_ctx"].rearrange("(r p) -> r p", p=P)).then_inc(rows_in, 16)
            sp.dma_start(rowt[80:116, :], t["conv_w"].rearrange("o t (r p) -> (o t r) p", p=P)).then_inc(rows_in, 16)
            sp.dma_start(dtb[:, :], t["dt_bias"].rearrange("o d h -> o (d h)").broadcast_to([P, 8])).then_inc(heads_in, 16)
            sp.dma_start(nega[:, :], t["a_log"].rearrange("o d h -> o (d h)").broadcast_to([P, 8])).then_inc(heads_in, 16)
            sp.wait_ge(zeroed, 1)
            for d in range(2):
                sp.dma_start(w2[16 * d:16 * d + 16, 256 * d:256 * d + 256], t["gla_w2"][0, d]).then_inc(small_in, 16)
            sp.dma_start(w2[32:33, :], t["gla_b"].rearrange("o d n -> o (d n)")).then_inc(small_in, 16)
            for g in range(2):
                sp.dma_start(wst[:, g, :, :], wmod_v[:, :, 512 * g:512 * g + 512]).then_inc(wmod_in[g], 16)
            sp.dma_start(xt[:, :, :], c_v).then_inc(x_in, 16)
            for g in range(2, 4):
                sp.wait_ge(mod_full, g - 1)
                sp.dma_start(wst[:, g % 2, :, :], wmod_v[:, :, 512 * g:512 * g + 512]).then_inc(wmod_in[g % 2], 16)
            for k in range(KD):
                sp.dma_start(win[:, k, :], win_v[:, k, :]).then_inc(w_in_in, 16)

            def load_x(hb):
                wait(sp, turn_full, 4 if isinstance(hb, int) and hb == 1 else 4 + (hb - 2) * NT + 6)
                sp.dma_start(xt[:, :, :], x_v[hb - 1]).then_inc(x_in, 16)

            def store(b, last):
                wait(sp, act_evac, 8 * (b + 1))
                wait(sp, turn_dve, 2 + NTV * (b + 1) - (2 if last else 0))
                sp.dma_start(rec_v[b], recb[:, :, :]).then_inc(rec_out, 16)

            load_x(1)
            store(0, False)
            with sp.Fori(0, 3) as i:
                for u in range(2):
                    load_x(2 * i + u + 2)
                    store(2 * i + u + 1, False)
            load_x(8)
            store(7, False)
            store(8, True)
            sp.wait_ge(rec_out, 16 * NBLK)

        @block.tensor
        def _(pe):
            pe.wait_ge(tab_in, 16)
            pe.wait_ge(rows_in, 96)
            pe.transpose(PT[0][:, 0:116], rowt[:, :], ident[0:116, 0:116]).then_inc(cols_full, 1)
            pe.wait_ge(silu_v, 3)
            for g in range(4):
                pe.wait_ge(wmod_in[g % 2], 16 * (g // 2 + 1))
                for j in range(4):
                    for k in range(KD):
                        mm = pe.matmul(PL[0][:, (4 * g + j) * 2:(4 * g + j) * 2 + 2], wst[:, g % 2, k, j * P:(j + 1) * P],
                                       silu_c[:, :, k], start=k == 0, stop=k == KD - 1)
                mm.then_inc(mod_full, 1)

            def turn_h(hb, b):
                pe.wait_ge(xs_done, hb + 1)
                for g in range(4):
                    if b is None:
                        bank_ = PT[g % 2]
                        if g >= 2:
                            wait(pe, turn_act if g % 2 == 0 else turn_dve, 1)
                    else:
                        bank_, _ = turn_at(b, f"H{g}")
                        turn_free(pe, b, f"H{g}")
                    for j in range(4):
                        k, i = 2 * g + j // 2, j % 2
                        mm = pe.transpose(bank_[:, j * P:(j + 1) * P], xt[:, i, k * P:(k + 1) * P], ident)
                    mm.then_inc(turn_full, 1)

            turn_h(0, None)
            pe.wait_ge(w_in_in, 16 * KD)
            pe.wait_ge(small_in, 16 * 3)

            def main(b, u, ctx_block, last):
                h = hT[:, u, :, :]

                def job(j):
                    job_gone(pe, b if j >= 4 else b - 1, j - 4 if j >= 4 else j + 12)
                    acc = PA[j % 4]
                    if j < 8:
                        for c in range(2):
                            for k in range(KD):
                                col0 = T_COLS[j] + c * P
                                mm = pe.matmul(acc[:, c * BT:(c + 1) * BT], win[:, k, col0:col0 + P], h[:, k, :],
                                               start=k == 0, stop=k == KD - 1)
                    elif j in (10, 11):
                        i = j - 10
                        for c0, n, o in ((W_BETA, 16, 0), (W_LR, 32, 16)):
                            for k in range(KD):
                                mm = pe.matmul(acc[:, o:o + n], h[:, k, i * P:(i + 1) * P], win[:, k, c0:c0 + n],
                                               start=k == 0, stop=k == KD - 1)
                    else:
                        i, c0, _ = TOK_JOBS[j]
                        for k in range(KD):
                            mm = pe.matmul(acc[:, :], h[:, k, i * P:(i + 1) * P], win[:, k, c0:c0 + 512],
                                           start=k == 0, stop=k == KD - 1)
                    mm.then_inc(job_full, 1)

                def turn(name, sources):
                    bank_, _ = turn_at(b, name, last)
                    turn_free(pe, b, name, last)
                    for s, src in enumerate(sources):
                        mm = pe.transpose(bank_[:, s * P:(s + 1) * P], src, ident)
                    mm.then_inc(turn_full, 1)

                if isinstance(b, int) and b == 0:
                    pe.wait_ge(turn_act, 2)
                    pe.wait_ge(turn_dve, 2)
                else:
                    turn_gone(pe, b - 1, "H2")
                    turn_gone(pe, b - 1, "H3")
                for j in range(8):
                    job(j)
                for i in range(4):
                    pe.wait_ge(sq_done, b * 4 + i + 1)
                    wait(pe, rs_done, b * 4 + i - 1)
                    pe.matmul(PL[i % 2][:, :], ones, sq[:, i % 2, :], start=True, stop=True).then_inc(l2_full, 1)
                for j in (8, 9, 10, 11):
                    job(j)
                pe.wait_ge(silu_done, b * 6 + 6)
                for i in range(2):
                    turn(f"V{i}", [ytmp[:, 8 + h_, i * P:(i + 1) * P] for h_ in range(4)])
                if not last:
                    turn_h(b + 1, b)
                job(12)
                pe.wait_ge(act_evac, b * 8 + 2)
                turn("BK", [recb[:, i, R_BK + c * P:R_BK + (c + 1) * P] for i in range(2) for c in range(2)])
                pe.wait_ge(qk_done, b * 4 + 4)
                for i in range(2):
                    turn(f"K{i}", [recb[:, i, R_KQ + 2 * h_ * P:R_KQ + (2 * h_ + 1) * P] for h_ in range(4)])
                job(13)
                bank_, _ = turn_at(b, "LR")
                turn_free(pe, b, "LR", last)
                pe.wait_ge(narrow_done, b * 2 + 2)
                for i in range(2):
                    mm = pe.transpose(bank_[0:32, i * P:(i + 1) * P], small[:, i, 16:48], ident)
                mm.then_inc(turn_full, 1)
                job(14)
                turn_gone(pe, b, "LR", last)
                for i in range(2):
                    bank_, _ = turn_at(b, f"G{i}")
                    turn_free(pe, b, f"G{i}", last)
                    pe.matmul(bank_[:, :], blrT[:, i * P:(i + 1) * P], w2[:, :], start=True, stop=True).then_inc(turn_full, 1)
                job(15)

            main(0, 0, True, False)
            with pe.Fori(0, 3) as i:
                for u in range(2):
                    main(2 * i + u + 1, (1 + u) % 2, False, False)
            main(7, 1, False, False)
            main(8, 0, False, True)

        @block.scalar
        def _(act):
            nc.scalar.preload_act_table_set("natural_log_exp_and_others")
            act.wait_ge(cols_done, 1)
            act.activation(silu_c[:, :, :], col[:, 64:80].rearrange("p (s k) -> p s k", s=2), ACT.Exp, scale=-1.0).then_inc(silu_a, 1)
            act.wait_ge(heads_in, 32)
            act.activation(nega[:, :], nega[:, :], ACT.Exp).then_inc(nega_a, 1)

            def stats(hb):
                act.wait_ge(x_in, 16 * (hb + 1))
                wait(act, qk_done, 4 * hb)
                wait(act, l2_full, 4 * hb)
                for i in range(TB):
                    if i:
                        act.wait_ge(ss_done, 2 * hb + 1)
                    act.activation(rs[:, :, :].rearrange("p a b -> p (a b)"), xt[:, i, :], ACT.Square,
                                   accum_out=ss[:, i:i + 1]).then_inc(ss_done, 1)
                act.wait_ge(ss_done, 2 * (hb + 1))
                wait(act, xs_done, hb)
                act.activation(rstd[:, :], ss[:, :], ACT.Ln, scale=1.0 / D, bias=eps[:, :]).then_inc(rstd_ln, 1)
                act.wait_ge(rstd_ln, hb + 1)
                act.activation(rstd[:, :], rstd[:, :], ACT.Exp, scale=-0.5).then_inc(rstd_done, 1)

            def evac_h(hb, g, bank_, s):
                for j in range(2):
                    k = 2 * g + j
                    ins = act.activation(hT[:, hb, k, :], bank_[:, j * BT:(j + 1) * BT], ACT.Identity,
                                         scale=gain[:, s, k:k + 1], bias=mod[:, k, s:s + 1])
                ins.then_inc(turn_act, 1)

            act.wait_ge(zeroed, 1)
            stats(0)
            act.wait_ge(mod_done, 3)
            for g in (0, 2):
                act.wait_ge(turn_full, g + 1)
                evac_h(0, g, PT[0], 1)

            def main(b, u, ctx_block, last):
                for j in range(6):
                    act.wait_ge(conv_done, b * 6 + j + 1)
                    y = ytmp[:, 2 * j:2 * j + 2, :]
                    act.activation(y, y, ACT.Silu).then_inc(silu_done, 1)
                act.preload_act_table_set("natural_log_exp_and_others")
                wait(act, rec_out, 16 * b)

                def to_rec(j):
                    act.wait_ge(job_full, b * 16 + j + 1)
                    if j < 8:
                        o = R_BQ if j == 6 else R_BK
                        dst = recb[:, :, o:o + 2 * P].rearrange("p t (c n) -> p c t n", c=2)
                        src = PA[j % 4][:, :].rearrange("p (c t n) -> p c t n", c=2, t=TB)
                        act.activation(dst, src, ACT.Copy, scale=0.125 if j == 6 else 1.0).then_inc(act_evac, 1)
                    else:
                        i, _, o = TOK_JOBS[j]
                        act.activation(recb[:, i, o:o + 512], PA[j % 4][:, :], ACT.Copy).then_inc(act_evac, 1)

                to_rec(6)
                to_rec(7)
                for i in range(4):
                    act.wait_ge(l2_full, b * 4 + i + 1)
                    wait(act, qk_done, b * 4 + i - 1)
                    act.activation(rs[:, i % 2, :], PL[i % 2][:, :], ACT.Ln, bias=eps[:, :]).then_inc(l2_ln, 1)
                    act.wait_ge(l2_ln, b * 4 + i + 1)
                    act.activation(rs[:, i % 2, :], rs[:, i % 2, :], ACT.Exp, scale=-0.5).then_inc(rs_done, 1)
                to_rec(8)
                to_rec(9)
                if not last:
                    stats(b + 1)

                def turned(name, dst):
                    bank_, full = turn_at(b, name, last)
                    act.wait_ge(turn_full, full)
                    act.activation(dst, bank_[:, :], ACT.Copy).then_inc(turn_act, 1)

                turned("V0", recb[:, 0, R_V:R_V + 512])
                if not last:
                    for g in (0, 2):
                        bank_, full = turn_at(b, f"H{g}")
                        act.wait_ge(turn_full, full)
                        evac_h(1 - u, g, bank_, 0)
                to_rec(12)
                bank_, full = turn_at(b, "BK", last)
                act.wait_ge(turn_full, full)
                act.activation(recb[:, :, R_BKTOK:R_BKTOK + 256], bank_[:, :].rearrange("p (t n) -> p t n", t=2), ACT.Copy).then_inc(turn_act, 1)
                act.wait_ge(narrow_done, b * 2 + 2)
                wait(act, gate_v, b * 6 + 1)
                act.activation(gate[:, 0, :, :], small[:, :, 0:8], ACT.Exp, scale=-1.0).then_inc(gate_a, 1)
                act.activation(gate[:, 2, :, :], gate[:, 1, :, :], ACT.Abs).then_inc(gate_a, 1)
                act.wait_ge(gate_a, b * 4 + 2)
                act.activation(gate[:, 2, :, :], gate[:, 2, :, :], ACT.Exp, scale=-1.0).then_inc(gate_a, 1)
                act.wait_ge(gate_a, b * 4 + 3)
                act.activation(gate[:, 2, :, :], gate[:, 2, :, :], ACT.Ln, bias=1.0).then_inc(gate_a, 1)
                bank_, full = turn_at(b, "K1", last)
                act.wait_ge(turn_full, full)
                act.activation(recb[:, 1, R_KTOK:R_KTOK + 512], bank_[:, :], ACT.Copy).then_inc(turn_act, 1)
                to_rec(13)
                to_rec(14)
                for i in range(2):
                    bank_, full = turn_at(b, f"G{i}", last)
                    act.wait_ge(turn_full, full)
                    if i == 0:
                        wait(act, qk_done, b * 4 + 4)
                    act.activation(rs[:, i, :], bank_[:, :], ACT.Abs).then_inc(gk_ln, 1)
                    act.wait_ge(gk_ln, b * 4 + 2 * i + 1)
                    act.activation(rs[:, i, :], rs[:, i, :], ACT.Exp, scale=-1.0).then_inc(gk_ln, 1)
                    act.wait_ge(gk_ln, b * 4 + 2 * i + 2)
                    act.activation(rs[:, i, :], rs[:, i, :], ACT.Ln, bias=1.0).then_inc(gk_a, 1)
                to_rec(15)

            main(0, 0, True, False)
            with act.Fori(0, 3) as i:
                for u in range(2):
                    main(2 * i + u + 1, (1 + u) % 2, False, False)
            main(7, 1, False, False)
            main(8, 0, False, True)

        @block.vector
        def _(dve):
            dve.memset(w2[:, :], 0.0)
            dve.memset(blrT[32:33, :], 1.0)
            dve.memset(eps[:, :], EPS).then_inc(zeroed, 1)
            dve.wait_ge(cols_full, 1)
            dve.tensor_copy(col[:, :], PT[0][:, 0:116]).then_inc(cols_done, 1)
            dve.wait_ge(silu_a, 1)
            dve.tensor_scalar(silu_c[:, :, :], silu_c[:, :, :], 1.0, None, ALU.add).then_inc(silu_v, 1)
            dve.wait_ge(silu_v, 1)
            dve.reciprocal(silu_c[:, :, :], silu_c[:, :, :]).then_inc(silu_v, 1)
            dve.wait_ge(silu_v, 2)
            dve.wait_ge(cols_done, 1)
            dve.tensor_tensor(silu_c[:, :, :], silu_c[:, :, :], col[:, 64:80].rearrange("p (s k) -> p s k", s=2), ALU.mult).then_inc(silu_v, 1)
            dve.wait_ge(nega_a, 1)
            dve.tensor_scalar(nega[:, :], nega[:, :], -1.0, None, ALU.mult).then_inc(nega_done, 1)
            dve.wait_ge(mod_full, 4)
            dve.tensor_tensor(mod[:, :, :], PL[0][:, 0:4 * KD].rearrange("p (c s) -> p c s", s=2), lanes(col[:, 0:2 * KD], 2), ALU.add).then_inc(mod_done, 1)
            dve.wait_ge(mod_done, 1)
            for s in range(2):
                dve.scalar_tensor_tensor(out=gain[:, s, :], in0=mod[:, KD:2 * KD, s], scalar=1.0, in1=col[:, 48:56], op0=ALU.add, op1=ALU.mult).then_inc(mod_done, 1)

            def scale_x(hb):
                dve.wait_ge(rstd_done, hb + 1)
                for i in range(TB):
                    ins = dve.tensor_scalar(xt[:, i, :], xt[:, i, :], rstd[:, i:i + 1], None, ALU.mult)
                ins.then_inc(xs_done, 1)

            def evac_h(hb, g, bank_, s):
                for j in range(2):
                    k = 2 * g + j
                    ins = dve.tensor_scalar(hT[:, hb, k, :], bank_[:, j * BT:(j + 1) * BT], gain[:, s, k:k + 1],
                                            mod[:, k, s:s + 1], ALU.mult, ALU.add)
                ins.then_inc(turn_dve, 1)

            dve.wait_ge(mod_done, 3)
            scale_x(0)
            for g in (1, 3):
                dve.wait_ge(turn_full, g + 1)
                evac_h(0, g, PT[1], 1)

            def main(b, u, ctx_block, last):
                n_rows, width = (1, BT) if ctx_block else (BT // GRID_W, GRID_W)
                for j in range(6):
                    dve.wait_ge(job_full, b * 16 + j + 1)
                    if j == 0:
                        wait(dve, sq_done, b * 4)
                    if j == 4:
                        bank_, full = turn_at(b - 1, "V1")
                        if not (isinstance(b, int) and b == 0):
                            wait(dve, turn_full, full)
                    for tap in (1, 0, 2):
                        for c in range(2):
                            ch = 2 * j + c
                            w = col[:, 80 + tap * 12 + ch:80 + tap * 12 + ch + 1]
                            u_ = PA[j % 4][:, c * BT:(c + 1) * BT].rearrange("p (r w) -> p r w", r=n_rows)
                            y = ytmp[:, ch, :].rearrange("p (r w) -> p r w", r=n_rows)
                            if tap == 1:
                                ins = dve.tensor_scalar(y, u_, w, None, ALU.mult)
                            elif tap == 0:
                                ins = dve.scalar_tensor_tensor(out=y[:, :, 1:width], in0=u_[:, :, 0:width - 1], scalar=w,
                                                               in1=y[:, :, 1:width], op0=ALU.mult, op1=ALU.add)
                            else:
                                ins = dve.scalar_tensor_tensor(out=y[:, :, 0:width - 1], in0=u_[:, :, 1:width], scalar=w,
                                                               in1=y[:, :, 0:width - 1], op0=ALU.mult, op1=ALU.add)
                        if tap == 2:
                            ins.then_inc(conv_done, 1)
                        else:
                            ins.then_inc(conv_step, 1)
                            dve.wait_ge(conv_step, b * 12 + 2 * j + (1 if tap == 1 else 2))
                wait(dve, rec_out, 16 * b)
                for i in range(4):
                    dve.wait_ge(rs_done, b * 4 + i + 1)
                    for c in range(2):
                        h_ = 2 * (i % 2) + c
                        o = R_KQ + (2 * h_ + (1 if i < 2 else 0)) * P
                        ins = dve.scalar_tensor_tensor(out=recb[:, :, o:o + P], in0=ytmp[:, 2 * i + c, :].rearrange("p (t n) -> p t n", t=2),
                                                       scalar=P ** -0.5 if i < 2 else 1.0,
                                                       in1=rs[:, i % 2, c * BT:(c + 1) * BT].rearrange("p (t n) -> p t n", t=2),
                                                       op0=ALU.mult, op1=ALU.mult)
                    ins.then_inc(qk_done, 1)
                for i in range(2):
                    dve.wait_ge(job_full, b * 16 + 11 + i)
                    if i == 0 and not (isinstance(b, int) and b == 0):
                        _, full = turn_at(b - 1, "LR")
                        dve.wait_ge(turn_full, full)
                    dve.tensor_copy(small[:, i, :], PA[(10 + i) % 4][:, 0:48]).then_inc(narrow_done, 1)
                if not last:
                    scale_x(b + 1)
                bank_, full = turn_at(b, "V1", last)
                dve.wait_ge(turn_full, full)
                dve.tensor_copy(recb[:, 1, R_V:R_V + 512], bank_[:, :]).then_inc(turn_dve, 1)
                if not last:
                    for g in (1, 3):
                        bank_, full = turn_at(b, f"H{g}")
                        dve.wait_ge(turn_full, full)
                        evac_h(1 - u, g, bank_, 0)
                dve.wait_ge(narrow_done, b * 2 + 2)
                wait(dve, gate_a, b * 4)
                dve.tensor_tensor(gate[:, 1, :, :], small[:, :, 8:16], rows(dtb[:, :], 2), ALU.add).then_inc(gate_v, 1)
                bank_, full = turn_at(b, "K0", last)
                dve.wait_ge(turn_full, full)
                dve.tensor_copy(recb[:, 0, R_KTOK:R_KTOK + 512], bank_[:, :]).then_inc(turn_dve, 1)
                dve.wait_ge(gate_a, b * 4 + 1)
                dve.tensor_scalar(gate[:, 0, :, :], gate[:, 0, :, :], 1.0, None, ALU.add).then_inc(gate_v, 1)
                dve.wait_ge(gate_v, b * 6 + 2)
                dve.reciprocal(gate[:, 0, :, :], gate[:, 0, :, :]).then_inc(gate_v, 1)
                dve.wait_ge(gate_v, b * 6 + 3)
                dve.tensor_scalar(recb[:, :, R_NB:R_NB + 8], gate[:, 0, :, :], -1.0, None, ALU.mult).then_inc(gate_v, 1)
                dve.wait_ge(gate_a, b * 4 + 4)
                dve.scalar_tensor_tensor(out=gate[:, 1, :, :], in0=gate[:, 1, :, :], scalar=0.0, in1=gate[:, 2, :, :], op0=ALU.max, op1=ALU.add).then_inc(gate_v, 1)
                dve.wait_ge(gate_v, b * 6 + 5)
                dve.tensor_tensor(recb[:, :, R_G:R_G + 8], gate[:, 1, :, :], rows(nega[:, :], 2), ALU.mult).then_inc(gate_v, 1)
                bank_, full = turn_at(b, "LR", last)
                dve.wait_ge(turn_full, full)
                dve.tensor_copy(blrT[0:32, :], bank_[0:32, 0:BT]).then_inc(turn_dve, 1)
                for i in range(2):
                    bank_, _ = turn_at(b, f"G{i}")
                    dve.wait_ge(gk_a, b * 2 + i + 1)
                    dve.scalar_tensor_tensor(out=recb[:, i, R_GK:R_GK + 512], in0=bank_[:, :], scalar=0.0, in1=rs[:, i, :],
                                             op0=ALU.min, op1=ALU.subtract).then_inc(turn_dve, 1)

            main(0, 0, True, False)
            with dve.Fori(0, 3) as i:
                for u in range(2):
                    main(2 * i + u + 1, (1 + u) % 2, False, False)
            main(7, 1, False, False)
            main(8, 0, False, True)

        @block.gpsimd
        def _(pool):
            def main(b):
                for i in range(4):
                    pool.wait_ge(silu_done, b * 6 + i + 1)
                    wait(pool, l2_full, b * 4 + i - 1)
                    y = ytmp[:, 2 * i:2 * i + 2, :].rearrange("p a b -> p (a b)")
                    pool.tensor_tensor(sq[:, i % 2, :], y, y, ALU.mult).then_inc(sq_done, 1)

            main(0)
            with pool.Fori(1, NBLK) as b:
                main(b)


def stage_mixers(nc, t, rec, mixed):
    steps_ctx, lat = CHUNKS_CTX, CHUNKS - CHUNKS_CTX
    dirs = (0, 1)
    with ExitStack() as ctx:
        sb = lambda name, shape, dt=F32: ctx.enter_context(nc.sbuf_tensor(name, shape, dt))
        two = lambda name, shape: [sb(f"{name}{d}", shape) for d in dirs]
        sem, clear = semaphores(nc)
        ctx.callback(clear)
        pair = lambda name: [sem(f"{name}_{s}") for s in ("fwd", "bwd")]
        tab = sb("tab3", [P, NTAB, P])
        masks = sb("masks3", [P, 2, NMASK, P], I8)
        ident = tab[:, C_ID, :]
        rin = [[sb(f"rin{d}{u}", [P, MIX]) for u in range(2)] for d in dirs]
        gsm, esm = two("gsm", [P, 12]), two("esm", [P, 12])
        decay = two("decay", [P, HA, P])
        resid = decay
        sysT = two("sysT", [P, HA, P])
        o_inter = sysT
        qkd = two("qkd", [P, HA, P])
        first_y = two("first_y", [P, HA, P])
        steps_t = [[sb(f"step{d}{l}", [P, HA, P]) for l in range(NLEV + 1)] for d in dirs]
        inv, invT = two("inv", [P, HA, P]), two("invT", [P, HA, P])
        v_dec = inv
        v_new = two("v_new", [P, HA, P])
        state_a = two("state_a", [P, HA, P])
        ex, exb, exm = two("ex", [P, 2, 4, P]), two("exb", [P, 512]), two("exm", [P, 256])
        ql, kl = two("ql", [P, 2, 2, 5, P]), two("kl", [P, 2, 4, P])
        k_dec, score = two("k_dec", [P, 256]), two("score", [P, HA, P])
        state_b = two("state_b", [P, 2, P])
        outb = two("outb", [P, 1024])
        BT_, BX, BY, BB = ([ctx.enter_context(nc.psum_tensor(f"{n}{d}", [P, 512], F32)) for d in dirs]
                           for n in ("bank_t", "bank_x", "bank_y", "bank_b"))
        by_head = lambda bank: bank[:, :].rearrange("p (h n) -> p h n", h=HA)

        tab_in, masks_in, masks_done, init_done = sem("tab_in3"), sem("masks_in3"), sem("masks_done"), sem("init_done")
        rec_in = [[sem(f"rec_in{d}{u}") for u in range(2)] for d in dirs]
        gc_full, gc_out, gr_full, dd_done, ddm_done, gl_done, esm_done, decay_done = map(
            pair, ("gc_full", "gc_out", "gr_full", "dd_done", "ddm_done", "gl_done", "esm_done", "decay_done"))
        kq_full, sys_done, qkd_done, sys_turned, first_done = map(pair, ("kq_full", "sys_done", "qkd_done", "sys_turned", "first_done"))
        t_full, t_done, x_full, x_out, y_full, y_out = map(pair, ("t_full", "t_done", "x_full", "x_out", "y_full", "y_out"))
        ks_full, r_done, qs_full, qs_out, z_full, vn_done, vd_done, oi_full, oa_done, su_full, s_done = map(
            pair, ("ks_full", "r_done", "qs_full", "qs_out", "z_full", "vn_done", "vd_done", "oi_full", "oa_done", "su_full", "s_done"))
        ex_full, ex_done, ql_done, kl_done, sc_full, sc_done, ob_full, ob_done, sub_full, bs_done, out_st = map(
            pair, ("ex_full", "ex_done", "ql_done", "kl_done", "sc_full", "sc_done", "ob_full", "ob_done", "sub_full", "bs_done", "out_st"))
        block = ctx.enter_context(nc.Block())

        both = lambda f, *a: [f(d, *a) for d in dirs]
        last = (P - 1, 0)
        const = lambda c, d: tab[:, c + d, :]
        w_cols = lambda d, a, b: tab[:, C_W + 5 * d + a:C_W + 5 * d + b, :].rearrange("p a b -> p (a b)")
        mask4 = lambda d, m: rows(masks[:, d, m, :], HA)

        @block.sync
        def _(sp):
            sp.dma_start(tab[:, :, :], t["table"].rearrange("p (a b) -> p a b", b=P)).then_inc(tab_in, 16)
            sp.dma_start(rin[1][1][:, 0:2 * NMASK * P], t["masks"]).then_inc(masks_in, 16)

            def load(d, n, u, chunk):
                sp.dma_start(rin[d][u][:, :], rec[chunk, :, 0:MIX]).then_inc(rec_in[d][u], 16)

            def store(d, n, chunks):
                chunk = chunks[d]
                sp.wait_ge(masks_in, 16)
                wait(sp, oa_done[d], n - 1)
                wait(sp, ob_done[d], n - 1)
                sp.dma_start(mixed[d, chunk], outb[d][:, :]).then_inc(out_st[d], 16)

            def load_next(d, n, u, chunks):
                sp.wait_ge(masks_in, 16)
                wait(sp, su_full[d], n + 1)
                wait(sp, sub_full[d], n + 1)
                load(d, n + 2, u, chunks[d])

            for n in range(2):
                if n == 1:
                    sp.wait_ge(masks_done, 1)
                load(0, n, n, n)
                load(1, n, n, steps_ctx - 1 - n)
            for n in range(2):
                both(load_next, n, n, (n + 2, CHUNKS - 1 - n))
            with sp.Fori(1, CHUNKS // 2 - 1) as i:
                for u in range(2):
                    n = 2 * i + u
                    both(store, n, (n - 2, CHUNKS - 1 - n))
                    both(load_next, n, u, (n + 2, CHUNKS - 1 - n))
            for n in (CHUNKS - 2, CHUNKS - 1):
                both(store, n, (n - 2, CHUNKS - 1 - n))
            for d in dirs:
                sp.wait_ge(out_st[d], 16 * lat)

        @block.tensor
        def _(pe):
            pe.wait_ge(tab_in, 16)

            def four(bank, lhs, rhs):
                for h in range(HA):
                    mm = pe.matmul(bank[:, h * P:(h + 1) * P], lhs(h), rhs(h), start=True, stop=True)
                return mm

            def gates(d, n, u, i):
                g = rin[d][u][:, R_G + 4 * d:R_G + 4 * d + 4]
                pe.wait_ge(rec_in[d][u], 16 * (i + 1))
                pe.wait_ge(s_done[d], n + 1)
                pe.matmul(BY[d][:, 0:4], const(C_TRI, d), g, start=True, stop=True).then_inc(gc_full[d], 1)
                wait(pe, vn_done[d], n)
                four(BT_[d], lambda h: g[:, h:h + 1].broadcast_to([P, P]), lambda h: const(C_TRI, d)).then_inc(gr_full[d], 1)

            def exponents(d, n, u, p):
                gk = rin[d][u][:, R_GK + 256 * d:R_GK + 256 * d + 256]
                if p == 0:
                    pe.wait_ge(bs_done[d], n + 1)
                else:
                    pe.wait_ge(ex_done[d], 3 * n + p)
                if p < 2:
                    mm = pe.matmul(BB[d][:, :], gk[:, p * P:(p + 1) * P], w_cols(d, 0, 4), start=True, stop=True)
                else:
                    for q in range(2):
                        pe.matmul(BB[d][:, q * P:(q + 1) * P], gk[:, q * P:(q + 1) * P], w_cols(d, 4, 5), start=True, stop=True)
                    mm = pe.matmul(BB[d][:, 256:512], const(C_SUF, d), gk, start=True, stop=True)
                mm.then_inc(ex_full[d], 1)

            def products(d, n, u):
                wait(pe, r_done[d], n)
                wait(pe, oa_done[d], n - 2)
                pe.wait_ge(gc_out[d], n + 1)
                for h in range(HA):
                    kq = rin[d][u][:, R_KQ + 2 * h * P:R_KQ + 2 * (h + 1) * P]
                    bank = BX[d] if h < 2 else BY[d]
                    mm = pe.matmul(bank[:, (h % 2) * 256:(h % 2) * 256 + 256], kq[:, 0:P], kq, start=True, stop=True)
                mm.then_inc(kq_full[d], 1)

            def turn(d, n):
                pe.wait_ge(sys_done[d], n + 1)
                pe.wait_ge(gl_done[d], n + 1)
                for h in range(HA):
                    mm = pe.transpose(BT_[d][:, h * P:(h + 1) * P], sysT[d][:, h, :], ident)
                mm.then_inc(sys_turned[d], 1)

            def level_t(d, n, l):
                x = steps_t[d][0] if l == 0 else inv[d]
                if l == 0:
                    pe.wait_ge(first_done[d], 2 * n + 2)
                else:
                    pe.wait_ge(x_out[d], 5 * n + l)
                four(BT_[d], lambda h: sysT[d][:, h, :], lambda h: x[:, h, :]).then_inc(t_full[d], 1)

            def level_xy(d, n, l):
                y = first_y[d] if l == 0 else invT[d]
                step = steps_t[d][l + 1]
                pe.wait_ge(t_done[d], NLEV * n + l + 1)
                if l == 0:
                    pe.wait_ge(qkd_done[d], n + 1)
                else:
                    pe.wait_ge(y_out[d], NLEV * n + l)
                if l < NLEV - 1:
                    four(BX[d], lambda h: y[:, h, :], lambda h: step[:, h, :]).then_inc(x_full[d], 1)
                four(BY[d], lambda h: step[:, h, :], lambda h: y[:, h, :]).then_inc(y_full[d], 1)

            def scores(d, n, v):
                if v == 0:
                    pe.wait_ge(ex_done[d], 3 * n + 3)
                    pe.wait_ge(ql_done[d], n + 1)
                    pe.wait_ge(kl_done[d], n + 1)
                else:
                    pe.wait_ge(sc_done[d], 4 * n + v)
                for p in range(2):
                    mm = pe.matmul(BB[d][:, p * 256:(p + 1) * 256], kl[d][:, p, v, :], ql[d][:, p, :, v + 1, :], start=True, stop=True)
                mm.then_inc(sc_full[d], 1)

            def out_b(d, n, u):
                bv = rin[d][u][:, R_BV:R_BV + 512]
                pe.wait_ge(sc_done[d], 4 * n + 4)
                for h in range(HA):
                    pe.matmul(BB[d][:, h * P:(h + 1) * P], score[d][:, h, :], bv[:, h * P:(h + 1) * P], start=True, stop=False)
                    mm = pe.matmul(BB[d][:, h * P:(h + 1) * P], ql[d][:, h // 2, h % 2, 0, :], state_b[d][:, h // 2, :], start=False, stop=True)
                mm.then_inc(ob_full[d], 1)

            def update_b(d, n, u, ctx_step):
                if ctx_step:
                    pe.wait_ge(sc_done[d], 4 * n + 4)
                else:
                    pe.wait_ge(ob_done[d], n - 1)
                for p in range(2):
                    mm = pe.matmul(BB[d][:, p * 256:(p + 1) * 256], k_dec[d][:, p * P:(p + 1) * P],
                                   rin[d][u][:, R_BV + 256 * p:R_BV + 256 * p + 256], start=True, stop=True)
                mm.then_inc(sub_full[d], 1)

            kT = lambda d, u, h: rin[d][u][:, R_KQ + 2 * h * P:R_KQ + (2 * h + 1) * P]
            qT = lambda d, u, h: rin[d][u][:, R_KQ + (2 * h + 1) * P:R_KQ + (2 * h + 2) * P]

            def state_k(d, n, u):
                pe.wait_ge(x_out[d], 5 * n + 5)
                four(BX[d], lambda h: kT(d, u, h), lambda h: state_a[d][:, h, :]).then_inc(ks_full[d], 1)

            def state_q(d, n, u):
                pe.wait_ge(r_done[d], n + 1)
                four(BX[d], lambda h: qT(d, u, h), lambda h: state_a[d][:, h, :]).then_inc(qs_full[d], 1)

            def solve(d, n):
                pe.wait_ge(r_done[d], n + 1)
                pe.wait_ge(y_out[d], NLEV * (n + 1))
                four(BT_[d], lambda h: invT[d][:, h, :], lambda h: resid[d][:, h, :]).then_inc(z_full[d], 1)

            def out_a(d, n):
                pe.wait_ge(vn_done[d], n + 1)
                pe.wait_ge(qs_out[d], n - 1)
                four(BX[d], lambda h: qkd[d][:, h, :], lambda h: v_new[d][:, h, :]).then_inc(oi_full[d], 1)

            def update_a(d, n, u):
                pe.wait_ge(vd_done[d], n + 1)
                four(BY[d], lambda h: rin[d][u][:, R_KTOK + h * P:R_KTOK + (h + 1) * P],
                     lambda h: v_dec[d][:, h, :]).then_inc(su_full[d], 1)

            def step(n, u, i, ctx_step):
                both(gates, n, u, i)
                both(exponents, n, u, 0)
                both(products, n, u)
                both(exponents, n, u, 1)
                both(turn, n)
                both(exponents, n, u, 2)
                for l in range(NLEV - 1):
                    both(level_t, n, l)
                    both(level_xy, n, l)
                    if l < 4:
                        both(scores, n, l)
                if not ctx_step:
                    both(out_b, n, u)
                both(level_t, n, NLEV - 1)
                both(update_b, n, u, ctx_step)
                both(state_k, n, u)
                both(level_xy, n, NLEV - 1)
                if not ctx_step:
                    both(state_q, n, u)
                both(solve, n)
                if not ctx_step:
                    both(out_a, n)
                both(update_a, n, u)

            for n in range(2):
                step(n, n, 0, True)
            with pe.Fori(1, CHUNKS // 2) as i:
                for u in range(2):
                    step(2 * i + u, u, i, False)

        @block.scalar
        def _(act):
            act.preload_act_table_set("natural_log_exp_and_others")

            def decays(d, n):
                act.wait_ge(gl_done[d], n + 1)
                act.wait_ge(s_done[d], n + 1)
                wait(act, vd_done[d], n)
                act.activation(esm[d][:, :], gsm[d][:, :], ACT.Exp).then_inc(esm_done[d], 1)
                act.wait_ge(ddm_done[d], n + 1)
                act.activation(decay[d][:, :, :], decay[d][:, :, :], ACT.Exp).then_inc(decay_done[d], 1)

            def exponentials(d, n, p):
                act.wait_ge(ex_full[d], 3 * n + p + 1)
                if p == 0:
                    wait(act, ql_done[d], n)
                    wait(act, kl_done[d], n)
                if p < 2:
                    act.activation(ex[d][:, p, :, :].rearrange("p a b -> p (a b)"), BB[d][:, :], ACT.Exp, scale=1 / NORMALIZER).then_inc(ex_done[d], 1)
                else:
                    act.activation(exm[d][:, :], BB[d][:, 0:256], ACT.Exp, scale=-1 / NORMALIZER)
                    act.activation(exb[d][:, :], BB[d][:, :], ACT.Exp, scale=1 / NORMALIZER).then_inc(ex_done[d], 1)

            def inverse_x(d, n, l):
                act.wait_ge(x_full[d], 5 * n + l + 1)
                act.activation(inv[d][:, :, :], by_head(BX[d]), ACT.Copy).then_inc(x_out[d], 1)

            def inverse_y(d, n, l):
                act.wait_ge(y_full[d], NLEV * n + l + 1)
                act.activation(invT[d][:, :, :], by_head(BY[d]), ACT.Copy).then_inc(y_out[d], 1)

            def copy_b(d, n):
                act.wait_ge(ob_full[d], n - 1)
                wait(act, out_st[d], 16 * (n - 2))
                act.activation(outb[d][:, 512:1024], BB[d][:, :], ACT.Copy).then_inc(ob_done[d], 1)

            def decay_q(d, n):
                act.wait_ge(qs_full[d], n - 1)
                act.wait_ge(esm_done[d], n + 1)
                for h in range(HA):
                    ins = act.activation(o_inter[d][:, h, :], BX[d][:, h * P:(h + 1) * P], ACT.Copy, scale=esm[d][:, h:h + 1])
                ins.then_inc(qs_out[d], 1)

            def step(n, u, ctx_step):
                both(decays, n)
                for p in range(3):
                    both(exponentials, n, p)
                for l in range(NLEV - 1):
                    for d in dirs:
                        inverse_x(d, n, l)
                        inverse_y(d, n, l)
                if not ctx_step:
                    both(copy_b, n)
                both(inverse_y, n, NLEV - 1)
                if not ctx_step:
                    both(decay_q, n)

            for n in range(2):
                step(n, n, True)
            with act.Fori(1, CHUNKS // 2) as i:
                for u in range(2):
                    step(2 * i + u, u, False)

        @block.vector
        def _(dve):
            for d in dirs:
                dve.memset(state_a[d][:, :, :], 0.0).then_inc(s_done[d], 1)
                dve.memset(state_b[d][:, :, :], 0.0).then_inc(bs_done[d], 1)
                dve.memset(score[d][:, :, :], 0.0)
            dve.wait_ge(tab_in, 16)
            for d in dirs:
                for x in (first_y[d], *steps_t[d]):
                    ins = dve.tensor_copy(x[:, :, :], rows(ident, HA))
            ins.then_inc(init_done, 1)
            dve.wait_ge(init_done, 1)
            dve.wait_ge(masks_in, 16)
            dve.tensor_copy(masks[:, :, :, :].rearrange("p d a b -> p (d a b)"), rin[1][1][:, 0:2 * NMASK * P]).then_inc(masks_done, 1)
            dve.wait_ge(masks_done, 1)

            def wait_apart(*pairs):
                values = [v if isinstance(v, int) else dve.to_reg(v) for v in pairs[1::2]]
                dve.wait_ge(tab_in, 16)
                for sem_, v in zip(pairs[::2], values):
                    wait(dve, sem_, v)

            def sums(d, n):
                g = gsm[d]
                dve.wait_ge(gc_full[d], n + 1)
                wait(dve, esm_done[d], n)
                dve.tensor_copy(g[:, 0:4], BY[d][:, 0:4]).then_inc(gc_out[d], 1)
                dve.wait_ge(gr_full[d], n + 1)
                dve.wait_ge(gc_out[d], n + 1)
                dve.tensor_tensor(decay[d][:, :, :], by_head(BT_[d]), lanes(g[:, 0:4], P), ALU.subtract).then_inc(dd_done[d], 1)
                dve.tensor_copy(g[:, 4:8], by_head(BT_[d])[:, :, last[d]])
                dve.tensor_tensor(g[:, 8:12], by_head(BT_[d])[:, :, last[d]], g[:, 0:4], ALU.subtract).then_inc(gl_done[d], 1)

            def system(d, n, u):
                nb = rin[d][u][:, R_NB + 4 * d:R_NB + 4 * d + 4]
                dve.wait_ge(kq_full[d], n + 1)
                dve.wait_ge(decay_done[d], n + 1)
                for h in range(HA):
                    kk = (BX, BY)[h // 2][d][:, (h % 2) * 256:(h % 2) * 256 + P]
                    ins = dve.scalar_tensor_tensor(out=sysT[d][:, h, :], in0=kk, scalar=nb[:, h:h + 1], in1=decay[d][:, h, :],
                                                   op0=ALU.mult, op1=ALU.mult)
                ins.then_inc(sys_done[d], 1)
                wait(dve, qkd_done[d], n)
                for j, bank in enumerate((BX[d], BY[d])):
                    kq = bank[:, :].rearrange("p (h a n) -> p h a n", h=2, a=2)[:, :, 1, :]
                    ins = dve.tensor_tensor(qkd[d][:, 2 * j:2 * j + 2, :], kq, decay[d][:, 2 * j:2 * j + 2, :], ALU.mult)
                ins.then_inc(qkd_done[d], 1)

            def first(d, n):
                wait_apart(sys_done[d], n + 1)
                dve.copy_predicated(first_y[d][:, :, :], mask4(d, M_FIRST_T), sysT[d][:, :, :]).then_inc(first_done[d], 1)
                wait_apart(sys_turned[d], n + 1)
                dve.copy_predicated(steps_t[d][0][:, :, :], mask4(d, M_LEV), by_head(BT_[d])).then_inc(first_done[d], 1)

            def decayed_k(d, n, u):
                bk = rin[d][u][:, R_BK:R_BK + 256]
                dve.wait_ge(ex_done[d], 3 * n + 3)
                for p in range(2):
                    dve.tensor_tensor(kl[d][:, p, 0:3, :], rows(bk[:, p * P:(p + 1) * P], 3), ex[d][:, p, 1:4, :], ALU.mult)
                dve.tensor_tensor(kl[d][:, :, 3, :], bk.rearrange("p (a b) -> p a b", a=2),
                                  exm[d][:, :].rearrange("p (a b) -> p a b", a=2), ALU.mult)
                dve.tensor_tensor(k_dec[d][:, :], rin[d][u][:, R_BKTOK:R_BKTOK + 256], exb[d][:, 256:512], ALU.mult).then_inc(kl_done[d], 1)

            def level(d, n, l):
                wait_apart(t_full[d], NLEV * n + l + 1)
                dve.copy_predicated(steps_t[d][l + 1][:, :, :], mask4(d, M_LEV + l + 1), by_head(BT_[d])).then_inc(t_done[d], 1)

            def mask_scores(d, n, v):
                wait_apart(sc_full[d], 4 * n + v + 1, sc_done[d], 4 * n + v)
                dve.copy_predicated(score[d][:, :, :], mask4(d, M_BLK + v), by_head(BB[d])).then_inc(sc_done[d], 1)

            def new_state_b(d, n):
                dve.wait_ge(sub_full[d], n + 1)
                for p in range(2):
                    for h in range(2):
                        r = slice(64 * h, 64 * h + 64)
                        ins = dve.scalar_tensor_tensor(out=state_b[d][r, p, :], in0=state_b[d][r, p, :], scalar=ex[d][r, p, 0, last[d]:last[d] + 1],
                                                       in1=BB[d][r, p * 256 + h * P:p * 256 + (h + 1) * P], op0=ALU.mult, op1=ALU.add)
                ins.then_inc(bs_done[d], 1)

            def residual(d, n, u):
                dve.wait_ge(ks_full[d], n + 1)
                dve.wait_ge(esm_done[d], n + 1)
                for h in range(HA):
                    ins = dve.scalar_tensor_tensor(out=resid[d][:, h, :], in0=BX[d][:, h * P:(h + 1) * P], scalar=esm[d][:, h:h + 1],
                                                   in1=rin[d][u][:, R_V + h * P:R_V + (h + 1) * P], op0=ALU.mult, op1=ALU.subtract)
                ins.then_inc(r_done[d], 1)

            def new_v(d, n, u):
                dve.wait_ge(z_full[d], n + 1)
                dve.tensor_tensor(v_new[d][:, :, :], by_head(BT_[d]), lanes(rin[d][u][:, R_NB + 4 * d:R_NB + 4 * d + 4], P), ALU.mult).then_inc(vn_done[d], 1)

            def add_a(d, n):
                dve.wait_ge(oi_full[d], n - 1)
                dve.wait_ge(qs_out[d], n - 1)
                wait(dve, out_st[d], 16 * (n - 2))
                dve.tensor_tensor(outb[d][:, 0:512].rearrange("p (h n) -> p h n", h=HA), by_head(BX[d]), o_inter[d][:, :, :], ALU.add).then_inc(oa_done[d], 1)

            def new_state_a(d, n):
                dve.wait_ge(su_full[d], n + 1)
                for h in range(HA):
                    ins = dve.scalar_tensor_tensor(out=state_a[d][:, h, :], in0=state_a[d][:, h, :], scalar=esm[d][:, 4 + h:5 + h],
                                                   in1=BY[d][:, h * P:(h + 1) * P], op0=ALU.mult, op1=ALU.add)
                ins.then_inc(s_done[d], 1)

            def step(n, u, ctx_step):
                both(sums, n)
                both(system, n, u)
                both(first, n)
                both(decayed_k, n, u)
                for l in range(NLEV - 1):
                    both(level, n, l)
                    if l < 4:
                        both(mask_scores, n, l)
                both(level, n, NLEV - 1)
                both(new_state_b, n)
                both(residual, n, u)
                both(new_v, n, u)
                if not ctx_step:
                    both(add_a, n)
                both(new_state_a, n)

            for n in range(2):
                step(n, n, True)
            with dve.Fori(1, CHUNKS // 2) as i:
                for u in range(2):
                    step(2 * i + u, u, False)

        @block.gpsimd
        def _(pool):
            for d in dirs:
                pool.memset(ql[d][:, :, :, :, :], 0.0)
            pool.wait_ge(tab_in, 16)

            def mask_decay(d, n):
                pool.wait_ge(dd_done[d], n + 1)
                pool.tensor_tensor(decay[d][:, :, :], decay[d][:, :, :], rows(const(C_NEG, d), HA), ALU.add).then_inc(ddm_done[d], 1)

            def decayed_q(d, n, u):
                pool.wait_ge(ex_done[d], 3 * n + 3)
                wait(pool, sub_full[d], n)
                for h in range(2):
                    r = slice(64 * h, 64 * h + 64)
                    for p in range(2):
                        pool.tensor_tensor(ql[d][r, p, h, 0:4, :], rows(rin[d][u][r, R_BQ + p * P:R_BQ + (p + 1) * P], 4), ex[d][r, p, :, :], ALU.mult)
                    ins = pool.tensor_tensor(ql[d][r, :, h, 4, :], rin[d][u][r, R_BQ:R_BQ + 256].rearrange("p (a b) -> p a b", a=2),
                                             exb[d][r, 0:256].rearrange("p (a b) -> p a b", a=2), ALU.mult)
                ins.then_inc(ql_done[d], 1)

            def decayed_v(d, n):
                pool.wait_ge(vn_done[d], n + 1)
                pool.wait_ge(esm_done[d], n + 1)
                pool.tensor_tensor(v_dec[d][:, :, :], v_new[d][:, :, :], lanes(esm[d][:, 8:12], P), ALU.mult).then_inc(vd_done[d], 1)

            def step(n, u):
                both(mask_decay, n)
                both(decayed_q, n, u)
                both(decayed_v, n)

            for n in range(2):
                step(n, n)
            with pool.Fori(1, CHUNKS // 2) as i:
                for u in range(2):
                    step(2 * i + u, u)


TILES = 4
NB = SEQ // P // TILES
G_PAIRS = FC // 2


def stage_ffn(nc, t, rec, mixed, out, col, silu_c):
    with ExitStack() as ctx:
        sb = lambda name, shape, dt=F32: ctx.enter_context(nc.sbuf_tensor(name, shape, dt))
        sem, clear = semaphores(nc)
        ctx.callback(clear)
        ident = sb("ident4", [P, P])
        wout = sb("wout", [P, KD, D])
        g1b, g2b, fin = sb("g1b", [P, D]), sb("g2b", [P, D]), sb("fin", [P, D])
        gain2, shift2 = sb("gain2", [P, KD]), sb("shift2", [P, KD])
        head_gain = sb("head_gain", [P, 2])
        eps = sb("eps4", [P, 1])
        ld = sb("ld", [P, 3, D])
        gated = sb("gated", [P, TILES, D])
        x1 = sb("x1", [P, TILES, D])
        hT = sb("hT4", [P, KD, TILES * P])
        hid = sb("hid", [P, FC, TILES * P])
        mixT = hid[:, 0:4, :].rearrange("p (u a) (b n) -> p u (a b) n", u=2, n=P)
        gu = [sb(f"gu{i}", [P, 2, KD, 256]) for i in range(2)]
        wst = [g[:, :, :, :].rearrange("p a k n -> p (a k n)").rearrange("p (k n) -> p k n", k=KD) for g in gu]
        wd = sb("wd", [P, 4, 512])
        sg = sb("sg", [P, 2, 512])
        scratch = sg[:, :, :].rearrange("p a b -> p (a b)")
        tmp = sb("tmp", [P, 2, 512])
        ss8, r8 = sb("ss8", [P, 8]), sb("r8", [P, 8])
        ss, rstd = sb("ss4", [P, TILES]), sb("rstd4", [P, TILES])
        GA = [ctx.enter_context(nc.psum_tensor(f"ga{i}", [P, 512], F32)) for i in range(4)]
        DN = [ctx.enter_context(nc.psum_tensor(f"dn{i}", [P, 512], F32)) for i in range(4)]

        const_in, wout_in, eps_done = sem("const_in"), sem("wout_in"), sem("eps_done")
        wmod_in = [sem(f"wmod_in4{i}") for i in range(2)]
        mod_full, mod_done, rows_done = sem("mod_full4"), sem("mod_done4"), sem("rows_done")
        ld_in, o_sum, o_sq, ss8_done, r8_ln, r8_done, z_silu, o_norm, gated_done = (
            sem("ld_in"), sem("o_sum"), sem("o_sq"), sem("ss8_done"), sem("r8_ln"), sem("r8_done"), sem("z_silu"), sem("o_norm"), sem("gated_done"))
        x_in, m_full, m_out, o_full, o_read, add_done = sem("x_in4"), sem("m_full"), sem("m_out"), sem("o_full"), sem("o_read"), sem("add_done")
        ss_done, st_ln, rstd_done, xn_done, h_full, h_act, h_dve = (
            sem("ss_done4"), sem("st_ln"), sem("rstd_done4"), sem("xn_done"), sem("h_full"), sem("h_act"), sem("h_dve"))
        gu_in = [sem(f"gu_in{i}") for i in range(2)]
        wd_in = [sem(f"wd_in{i}") for i in range(4)]
        gate_full, up_full, sg_done, hid_done, wd_used, dn_full = sem("gate_full"), sem("up_full"), sem("sg_done"), sem("hid_done"), sem("wd_used"), sem("dn_full")
        y_norm, y_done, y_out = sem("y_norm"), sem("y_done"), sem("y_out")
        block = ctx.enter_context(nc.Block())

        x_v = t["x"].rearrange("o (b t p) d -> (o b) p t d", t=TILES, p=P)
        out_v = out.rearrange("o (b t p) d -> (o b) p t d", t=TILES, p=P)
        wmod_v = t["w_mod"].rearrange("o (k p) n -> (o p) k n", p=P)
        wg_v = t["w_gate"].rearrange("o (k p) n -> (o p) k n", p=P)
        wu_v = t["w_up"].rearrange("o (k p) n -> (o p) k n", p=P)
        wd_v = t["w_down"].rearrange("o (f p) n -> (o p) f n", p=P)
        pieces = [3 * D, 3 * D + 512, 4 * D, 4 * D + 512, 2 * D, 2 * D + 512, 5 * D, 5 * D + 512]
        GATE_AT = {3: 0, 8: 1, 13: 2, 18: 3}

        @block.sync
        def _(sp):
            sp.dma_start(ident[:, :], t["table"][:, 0:P]).then_inc(const_in, 16)
            for n, name in enumerate(("gdn_norm", "gla_norm")):
                sp.dma_start(head_gain[:, n:n + 1], t[name].rearrange("o p -> p o")).then_inc(const_in, 16)
            sp.dma_start(fin[:, :], t["final_norm"].unsqueeze(0).broadcast_to([P, D])).then_inc(const_in, 16)
            for g, c in ((g1b, 2 * D), (g2b, 5 * D)):
                sp.dma_start(g[:, :], t["b_mod"][:, c:c + D].broadcast_to([P, D])).then_inc(const_in, 16)

            def held(*pairs):
                values = [v if isinstance(v, int) else sp.to_reg(v) for v in pairs[1::2]]
                sp.wait_ge(const_in, 96)
                for sem_, v in zip(pairs[::2], values):
                    wait(sp, sem_, v)

            def load_tile(T):
                held(gated_done, T)
                for d in range(2):
                    sp.dma_start(ld[:, d, :], mixed[d, T]).then_inc(ld_in, 16)
                sp.dma_start(ld[:, 2, :], rec[T + CHUNKS_CTX, :, R_Z:REC]).then_inc(ld_in, 16)

            load_tile(0)
            for i, c in enumerate(pieces):
                if i >= 2:
                    sp.wait_ge(mod_full, i - 1)
                sp.dma_start(wst[i % 2], wmod_v[:, :, c:c + 512]).then_inc(wmod_in[i % 2], 16)
            for k in range(KD):
                sp.dma_start(wout[:, k, :], t["w_out"][0, k * P:(k + 1) * P, :]).then_inc(wout_in, 16)
            for T in range(1, TILES):
                load_tile(T)

            def load_gu(b, q):
                if q >= 2:
                    held(up_full, FC * b + 2 * q - 2)
                else:
                    held(up_full, FC * b)
                for m, w in enumerate((wg_v, wu_v)):
                    sp.dma_start(gu[q % 2][:, m, :, :], w[:, :, 256 * q:256 * q + 256]).then_inc(gu_in[q % 2], 16)

            def load_wd(b, j):
                half, f = j // FC, j % FC
                if j >= 4:
                    half_, f_ = (j - 4) // FC, (j - 4) % FC
                    if f_ < FC - 1:
                        held(wd_used, 2 * (FC - 1) * b + half_ * (FC - 1) + f_ + 1)
                    else:
                        held(dn_full, 8 * b + 4)
                else:
                    held(wd_used, 2 * (FC - 1) * b, dn_full, 8 * b)
                sp.dma_start(wd[:, j % 4, :], wd_v[:, f, 512 * half:512 * half + 512]).then_inc(wd_in[j % 4], 16)

            def main(b, last):
                held(y_out, 16 * TILES * b)
                sp.dma_start(x1[:, :, :], x_v[b]).then_inc(x_in, 16)
                for q in range(2, G_PAIRS):
                    load_gu(b, q)
                    if q in (3, 5, 7, 9) and not last:
                        load_tile(TILES * (b + 1) + (q - 3) // 2)
                for j in range(2 * FC):
                    load_wd(b, j)
                    if j == 12 and not last:
                        load_gu(b + 1, 0)
                        load_gu(b + 1, 1)
                for i in range(TILES):
                    held(y_done, TILES * b + i + 1)
                    sp.dma_start(out_v[b, :, i, :], x1[:, i, :]).then_inc(y_out, 16)

            sp.wait_ge(mod_full, 8)
            load_gu(0, 0)
            load_gu(0, 1)
            with sp.Fori(0, NB - 1) as b:
                main(b, False)
            main(NB - 1, True)
            sp.wait_ge(y_out, 16 * TILES * NB)

        @block.tensor
        def _(pe):
            pe.wait_ge(const_in, 96)
            for g in range(4):
                pe.wait_ge(wmod_in[g % 2], 16 * (g // 2 + 1))
                for j in range(4):
                    for k in range(KD):
                        mm = pe.matmul(DN[0][:, 4 * g + j:4 * g + j + 1], wst[g % 2][:, k, j * P:(j + 1) * P], silu_c[:, 0, k:k + 1],
                                       start=k == 0, stop=k == KD - 1)
                mm.then_inc(mod_full, 1)
            for g in range(4, 8):
                pe.wait_ge(wmod_in[g % 2], 16 * (g // 2 + 1))
                for k in range(KD):
                    mm = pe.matmul(GA[g - 4][:, :], silu_c[:, 0, k:k + 1].broadcast_to([P, P]), wst[g % 2][:, k, :],
                                   start=k == 0, stop=k == KD - 1)
                mm.then_inc(mod_full, 1)
            pe.wait_ge(rows_done, 4)
            pe.wait_ge(mod_done, 3)
            pe.wait_ge(wout_in, 16 * KD)

            def turn_mixed(b, i):
                T = TILES * b + i
                pe.wait_ge(gated_done, T + 1)
                wait(pe, m_out, T)
                if i == 0:
                    wait(pe, hid_done, FC * b)
                for k in range(KD):
                    mm = pe.transpose(GA[k // 4][:, (k % 4) * P:(k % 4 + 1) * P], gated[:, i, k * P:(k + 1) * P], ident[:, :])
                mm.then_inc(m_full, 1)

            def project(b, i):
                T = TILES * b + i
                pe.wait_ge(m_out, T + 1)
                for half in range(2):
                    wait(pe, o_read, 16 * b + 2 * i + half - 3 if i >= 2 else 16 * b)
                    for k in range(KD):
                        mm = pe.matmul(DN[2 * (i % 2) + half][:, :], mixT[:, i % 2, k, :], wout[:, k, half * 512:half * 512 + 512],
                                       start=k == 0, stop=k == KD - 1)
                    mm.then_inc(o_full, 1)

            def turn_norm(b, i):
                T = TILES * b + i
                pe.wait_ge(xn_done, T + 1)
                wait(pe, h_act, T)
                wait(pe, h_dve, T)
                for k in range(KD):
                    mm = pe.transpose(GA[2 + k // 4][:, (k % 4) * P:(k % 4 + 1) * P], gated[:, i, k * P:(k + 1) * P], ident[:, :])
                mm.then_inc(h_full, 1)

            def main(b, last):
                for s in range(TILES + 2):
                    if s < TILES:
                        turn_mixed(b, s)
                    if 1 <= s <= TILES:
                        project(b, s - 1)
                    if s >= 2:
                        turn_norm(b, s - 2)
                pe.wait_ge(h_act, TILES * (b + 1))
                pe.wait_ge(h_dve, TILES * (b + 1))
                for f in range(FC):
                    q = f // 2
                    if f % 2 == 0:
                        n = (G_PAIRS + 1) // 2 if q % 2 == 0 else G_PAIRS // 2
                        pe.wait_ge(gu_in[q % 2], 32 * (n * b + q // 2 + 1))
                    if f >= 2:
                        pe.wait_ge(hid_done, FC * b + f - 1)
                    for m in range(2):
                        for k in range(KD):
                            mm = pe.matmul(GA[2 * (f % 2) + m][:, :], gu[q % 2][:, m, k, (f % 2) * P:(f % 2 + 1) * P], hT[:, k, :],
                                           start=k == 0, stop=k == KD - 1)
                        mm.then_inc(up_full if m else gate_full, 1)
                for half in range(2):
                    pe.wait_ge(o_read, 16 * b + (8 if half == 0 else 12))
                    for f in range(FC):
                        j = half * FC + f
                        pe.wait_ge(wd_in[j % 4], 16 * (11 * b + j // 4 + 1))
                        pe.wait_ge(hid_done, FC * b + f + 1)
                        for i in range(TILES):
                            mm = pe.matmul(DN[i][:, :], hid[:, f, i * P:(i + 1) * P], wd[:, j % 4, :], start=f == 0, stop=f == FC - 1)
                            if f == FC - 1:
                                mm.then_inc(dn_full, 1)
                        if f < FC - 1:
                            mm.then_inc(wd_used, 1)

            with pe.Fori(0, NB - 1) as b:
                main(b, False)
            main(NB - 1, True)

        @block.scalar
        def _(act):
            def table_ln_exp():
                act.preload_act_table_set("natural_log_exp_and_others")

            def gate(T):
                act.wait_ge(ld_in, 48 * (T + 1))
                act.activation(ld[:, 2, :], ld[:, 2, :], ACT.Silu).then_inc(z_silu, 1)
                table_ln_exp()
                act.wait_ge(ss8_done, T + 1)
                wait(act, o_norm, T)
                act.activation(r8[:, :], ss8[:, :], ACT.Ln, scale=1.0 / P, bias=eps[:, :]).then_inc(r8_ln, 1)
                act.wait_ge(r8_ln, T + 1)
                act.activation(r8[:, :], r8[:, :], ACT.Exp, scale=-0.5).then_inc(r8_done, 1)

            def stats(i, n):
                wait(act, ss_done, n)
                act.activation(scratch, x1[:, i, :], ACT.Square, accum_out=ss[:, i:i + 1]).then_inc(ss_done, 1)
                act.wait_ge(ss_done, n + 1)
                act.activation(rstd[:, i:i + 1], ss[:, i:i + 1], ACT.Ln, scale=1.0 / D, bias=eps[:, :]).then_inc(st_ln, 1)
                act.wait_ge(st_ln, n + 1)
                act.activation(rstd[:, i:i + 1], rstd[:, i:i + 1], ACT.Exp, scale=-0.5).then_inc(rstd_done, 1)

            act.wait_ge(eps_done, 1)
            gate(0)
            act.wait_ge(const_in, 96)
            for T in range(1, TILES):
                gate(T)

            def mixed_out(b, i):
                T = TILES * b + i
                act.wait_ge(m_full, T + 1)
                wait(act, o_full, 8 * b + 2 * (i - 1) if i >= 2 else 8 * b)
                for g in range(2):
                    ins = act.activation(mixT[:, i % 2, 4 * g:4 * g + 4, :], GA[g][:, :].rearrange("p (a b) -> p a b", b=P), ACT.Copy,
                                         scale=head_gain[:, g:g + 1])
                ins.then_inc(m_out, 1)

            def norm_out(b, i):
                T = TILES * b + i
                act.wait_ge(h_full, T + 1)
                for k in range(4):
                    ins = act.activation(hT[:, k, i * P:(i + 1) * P], GA[2][:, k * P:(k + 1) * P], ACT.Identity,
                                         scale=gain2[:, k:k + 1], bias=shift2[:, k:k + 1])
                ins.then_inc(h_act, 1)

            def main(b, last):
                wait(act, dn_full, 8 * b)
                for s in range(TILES + 2):
                    if s < TILES:
                        mixed_out(b, s)
                    if s >= 2:
                        norm_out(b, s - 2)
                    if 1 <= s <= TILES:
                        act.wait_ge(add_done, 16 * b + 2 * s)
                        stats(s - 1, 8 * b + s - 1)
                for f in range(FC):
                    act.wait_ge(gate_full, FC * b + f + 1)
                    if f >= 2:
                        act.wait_ge(hid_done, FC * b + f - 1)
                    elif f == 0:
                        act.wait_ge(ss_done, 8 * b + 4)
                    act.activation(sg[:, f % 2, :], GA[2 * (f % 2)][:, :], ACT.Silu).then_inc(sg_done, 1)
                    if f in GATE_AT and not last:
                        gate(TILES * (b + 1) + GATE_AT[f])
                table_ln_exp()
                act.wait_ge(hid_done, FC * (b + 1))
                for i in range(TILES):
                    act.wait_ge(add_done, 16 * b + 8 + 4 + i + 1)
                    stats(i, 8 * b + 4 + i)

            with act.Fori(0, NB - 1) as b:
                main(b, False)
            main(NB - 1, True)

        @block.vector
        def _(dve):
            dve.memset(eps[:, :], EPS).then_inc(eps_done, 1)

            def gate(T, i):
                dve.wait_ge(o_sq, T + 1)
                wait(dve, r8_done, T)
                dve.tensor_reduce(ss8[:, :], ld[:, 1, :].rearrange("p (h n) -> p h n", n=P), AX.X, ALU.add).then_inc(ss8_done, 1)
                dve.wait_ge(r8_done, T + 1)
                o = ld[:, 0, :].rearrange("p (h n) -> p h n", n=P)
                dve.tensor_tensor(o, o, lanes(r8[:, :], P), ALU.mult).then_inc(o_norm, 1)
                dve.wait_ge(o_norm, T + 1)
                dve.wait_ge(z_silu, T + 1)
                dve.tensor_tensor(gated[:, i, :], ld[:, 0, :], ld[:, 2, :], ALU.mult).then_inc(gated_done, 1)

            gate(0, 0)
            dve.wait_ge(const_in, 96)
            dve.wait_ge(mod_full, 4)
            dve.tensor_tensor(shift2[:, :], DN[0][:, 0:KD], col[:, 3 * KD:4 * KD], ALU.add).then_inc(mod_done, 1)
            dve.tensor_tensor(gain2[:, :], DN[0][:, KD:2 * KD], col[:, 4 * KD:5 * KD], ALU.add).then_inc(mod_done, 1)
            dve.wait_ge(mod_done, 2)
            dve.scalar_tensor_tensor(out=gain2[:, :], in0=gain2[:, :], scalar=1.0, in1=col[:, 56:64], op0=ALU.add, op1=ALU.mult).then_inc(mod_done, 1)
            for n, (g, half) in enumerate(((g1b, 0), (g1b, 1), (g2b, 0), (g2b, 1))):
                dve.wait_ge(mod_full, 5 + n)
                r = g[:, half * 512:half * 512 + 512]
                dve.tensor_tensor(r, GA[n][:, :], r, ALU.add).then_inc(rows_done, 1)
            dve.wait_ge(rows_done, 4)
            for T in range(1, TILES):
                gate(T, T)

            def scaled(b, n, bank, g, half):
                wait(dve, add_done, 16 * b + max(n - 1, 0))
                dve.tensor_tensor(tmp[:, n % 2, :], bank[:, :], g[:, half * 512:half * 512 + 512], ALU.mult).then_inc(o_read, 1)

            def projected(b, i):
                for half in range(2):
                    dve.wait_ge(o_full, 8 * b + 2 * i + half + 1)
                    scaled(b, 2 * i + half, DN[2 * (i % 2) + half], g1b, half)

            def normalized(b, i):
                dve.wait_ge(rstd_done, 8 * b + i + 1)
                dve.tensor_scalar(gated[:, i, :], x1[:, i, :], rstd[:, i:i + 1], None, ALU.mult).then_inc(xn_done, 1)

            def norm_out(b, i):
                dve.wait_ge(h_full, TILES * b + i + 1)
                for k in range(4, KD):
                    ins = dve.tensor_scalar(hT[:, k, i * P:(i + 1) * P], GA[3][:, (k - 4) * P:(k - 3) * P], gain2[:, k:k + 1],
                                            shift2[:, k:k + 1], ALU.mult, ALU.add)
                ins.then_inc(h_dve, 1)

            def main(b, last):
                for i in range(TILES):
                    projected(b, i)
                    if i >= 1:
                        norm_out(b, i - 1)
                    normalized(b, i)
                norm_out(b, TILES - 1)
                for f in range(FC):
                    dve.wait_ge(up_full, FC * b + f + 1)
                    dve.wait_ge(sg_done, FC * b + f + 1)
                    dve.tensor_tensor(hid[:, f, :], GA[2 * (f % 2) + 1][:, :], sg[:, f % 2, :], ALU.mult).then_inc(hid_done, 1)
                    if f in GATE_AT and not last:
                        gate(TILES * (b + 1) + GATE_AT[f], GATE_AT[f])
                for half in range(2):
                    for i in range(TILES):
                        dve.wait_ge(dn_full, 8 * b + 4 * half + i + 1)
                        scaled(b, 8 + 4 * half + i, DN[i], g2b, half)
                for i in range(TILES):
                    dve.wait_ge(rstd_done, 8 * b + 4 + i + 1)
                    dve.tensor_scalar(x1[:, i, :], x1[:, i, :], rstd[:, i:i + 1], None, ALU.mult).then_inc(y_norm, 1)

            with dve.Fori(0, NB - 1) as b:
                main(b, False)
            main(NB - 1, True)

        @block.gpsimd
        def _(pool):
            def gate(T):
                pool.wait_ge(ld_in, 48 * (T + 1))
                pool.tensor_tensor(ld[:, 0, :], ld[:, 0, :], ld[:, 1, :], ALU.add).then_inc(o_sum, 1)
                pool.wait_ge(o_sum, T + 1)
                pool.tensor_tensor(ld[:, 1, :], ld[:, 0, :], ld[:, 0, :], ALU.mult).then_inc(o_sq, 1)

            for T in range(TILES):
                gate(T)

            def add(b, n, i, half):
                pool.wait_ge(o_read, 16 * b + n + 1)
                x = x1[:, i, half * 512:half * 512 + 512]
                pool.tensor_tensor(x, x, tmp[:, n % 2, :], ALU.add).then_inc(add_done, 1)

            def main(b, last):
                pool.wait_ge(x_in, 16 * (b + 1))
                for i in range(TILES):
                    for half in range(2):
                        add(b, 2 * i + half, i, half)
                if not last:
                    for i in range(TILES):
                        gate(TILES * (b + 1) + i)
                for half in range(2):
                    for i in range(TILES):
                        if half == 0:
                            pool.wait_ge(xn_done, TILES * b + i + 1)
                        add(b, 8 + 4 * half + i, i, half)
                for i in range(TILES):
                    pool.wait_ge(y_norm, TILES * b + i + 1)
                    pool.tensor_tensor(x1[:, i, :], x1[:, i, :], fin[:, :], ALU.mult).then_inc(y_done, 1)

            with pool.Fori(0, NB - 1) as b:
                main(b, False)
            main(NB - 1, True)


def layer(nc, t, out):
    rec = nc.dram_tensor("records", [CHUNKS, P, REC], F32, kind="Internal").ap()
    mixed = nc.dram_tensor("mixed", [2, CHUNKS - CHUNKS_CTX, P, 1024], F32, kind="Internal").ap()
    with ExitStack() as ctx:
        col = ctx.enter_context(nc.sbuf_tensor("col", [P, 116], F32))
        silu_c = ctx.enter_context(nc.sbuf_tensor("silu_c", [P, 2, KD], F32))
        stage_project(nc, t, rec, col, silu_c)
        stage_mixers(nc, t, rec, mixed)
        stage_ffn(nc, t, rec, mixed, out, col, silu_c)


INS = ["x", "c", "ctx", "c_ctx", "w_mod", "b_mod", "attn_norm", "w_in", "conv_w", "a_log", "dt_bias", "gdn_norm",
       "gla_w2", "gla_b", "gla_norm", "w_out", "ffn_norm", "w_gate", "w_up", "w_down", "final_norm"]


def kernel(**inputs):
    import numpy as _np
    import concourse.bacc as _bacc
    from concourse import mybir as _mybir
    from concourse.bass_utils import run_bass_kernel_spmd as _run

    nc = _bacc.Bacc("TRN2", target_bir_lowering=False, num_devices=1)
    arrays, args = {}, {}
    table, masks = tables()
    for name in [*INS, "table", "masks"]:
        a = _np.ascontiguousarray({"table": table, "masks": masks}[name] if name in ("table", "masks") else inputs[name])
        arrays[f"in_{name}_dram"] = a
        args[name] = nc.dram_tensor(f"in_{name}_dram", a.shape, _mybir.dt.from_np(a.dtype), kind="ExternalInput").ap()
    out = nc.dram_tensor("out_0_dram", (1, SEQ, D), F32, kind="ExternalOutput").ap()
    layer(nc, args, out)
    r = _run(nc, [arrays], core_ids=[0])
    return r.results[0]["out_0_dram"]
```

```python
from contextlib import ExitStack

import numpy as np

import concourse.bass as bass
from concourse import mybir

F32 = mybir.dt.float32
F32R = mybir.dt.float32r
I8 = mybir.dt.int8
ACT = mybir.ActivationFunctionType
ALU = mybir.AluOpType
AX = mybir.AxisListType

P = 128
D = 1024
KD = D // P
SEQ, CTX = 2048, 256
EPS = 1e-6
HA = 4
DFF = 2816
FC = DFF // P
IN_COLS = 3632
GRID_W = 64
CONV_K = 3
NORMALIZER = 16.0
CHUNKS_CTX, CHUNKS = CTX // P, (CTX + SEQ) // P
W_Q, W_K, W_V, W_Z, W_BETA, W_BQ, W_BK, W_BV, W_BG, W_LR = 0, 512, 1024, 1536, 2048, 2064, 2320, 2576, 3088, 3600

R_KQ = 0
R_BQ = R_KQ + 2 * HA * P
R_BK = R_BQ + 2 * P
R_KTOK = R_BK + 2 * P
R_V = R_KTOK + 512
R_BV = R_V + 512
R_BKTOK = R_BV + 512
R_NB = R_BKTOK + 256
R_G = R_NB + 8
R_GK = R_G + 8
MIX = R_GK + 512
R_Z = MIX
R_BG = R_Z + 512
REC = R_BG + 512

SIZES = [1, 2, 4, 8, 16, 32, 64]
BLOCKS = [64, 32, 16]
NLEV = len(SIZES) - 1

C_ID, C_ONE, C_TRI, C_SUF, C_NEG, C_W = 0, 1, 2, 4, 6, 8
NTAB = C_W + 2 * (len(BLOCKS) + 2)
M_LEV, M_FIRST_T, M_BLK = 0, len(SIZES), len(SIZES) + 1
NMASK = M_BLK + len(BLOCKS) + 1


def tables():
    t = np.arange(P)
    a, b = t[:, None], t[None, :]
    tri = (a <= b).astype(np.float32)
    suf = (a > b).astype(np.float32)
    neg = np.where(b >= a, 0.0, -1e30).astype(np.float32)
    w = [tri]
    blk = []
    for s in BLOCKS:
        r = b // (2 * s) * 2 * s + s - 1
        w.append(np.where(b > r, (a > r) & (a <= b), (a > b) & (a <= r)).astype(np.float32))
        blk.append((a // (2 * s) == b // (2 * s)) & (b // s % 2 == 1) & (a // s % 2 == 0))
    s = BLOCKS[-1]
    m = b // s * s + s // 2 - 1
    w.append(((a > m) & (a <= b)).astype(np.float32) - ((a > b) & (a <= m)).astype(np.float32))
    blk.append((a // s == b // s) & (b >= a))
    lev = [(a // (2 * s) == b // (2 * s)) & (a // s % 2 == 1) & (b // s % 2 == 0) for s in SIZES]
    masks = [x.astype(np.float32) for x in [*lev, lev[0].T, *blk]]
    both = lambda x: [x, x[::-1, ::-1]]
    cols = [np.eye(P, dtype=np.float32), np.ones((P, P), np.float32), *both(tri), *both(suf), *both(neg)]
    cols += [x for x in w] + [x[::-1, ::-1] for x in w]
    mcols = [x for x in masks] + [x[::-1, ::-1] for x in masks]
    return (np.ascontiguousarray(np.concatenate(cols, 1), dtype=np.float32),
            np.ascontiguousarray(np.concatenate(mcols, 1), dtype=np.float32))


def wait(eng, sem, value):
    if not (isinstance(value, int) and value <= 0):
        eng.wait_ge(sem, value)


def semaphores(nc):
    made = []

    def sem(name):
        made.append(nc.alloc_semaphore(name))
        return made[-1]

    def clear():
        nc.clear_and_free_semaphores(made)
        nc.all_engine_barrier()

    return sem, clear


def rows(ap, n):
    return ap.unsqueeze(1).broadcast_to([ap.shape[0], n, ap.shape[1]])


def lanes(ap, n):
    return ap.unsqueeze(2).broadcast_to([ap.shape[0], ap.shape[1], n])


TB = 2
BT = TB * P
NBLK = (CTX + SEQ) // BT
T_COLS = [W_Q, W_Q + 256, W_K, W_K + 256, W_V, W_V + 256, W_BQ, W_BK]
TOK_JOBS = {8: (0, W_Z, R_Z), 9: (0, W_BG, R_BG), 12: (0, W_BV, R_BV),
            13: (1, W_Z, R_Z), 14: (1, W_BG, R_BG), 15: (1, W_BV, R_BV)}
W_PARTS = {0: (W_Q, W_K), 2: (W_K, W_V), 4: (W_V, W_Z), 6: (W_BETA, W_BV), 8: (W_Z, W_BETA), 9: (W_BG, IN_COLS), 12: (W_BV, W_BG)}
TURNS = ["V0", "V1", "H0", "H1", "H2", "H3", "BK", "K0", "K1", "LR", "G0", "G1"]
BY_ACT = ["V0", "H0", "H2", "BK", "K1"]
BY_DVE = ["V1", "H1", "H3", "K0", "LR", "G0", "G1"]
NT, NTA, NTV = len(TURNS), len(BY_ACT), len(BY_DVE)


def stage_project(nc, t, rec, col, silu_c):
    with ExitStack() as ctx:
        sb = lambda name, shape, dt=F32: ctx.enter_context(nc.sbuf_tensor(name, shape, dt))
        bank = lambda name: ctx.enter_context(nc.psum_tensor(name, [P, 512], F32))
        sem, clear = semaphores(nc)
        ctx.callback(clear)
        tab = sb("tab", [P, 2, P])
        ident, ones = tab[:, 0, :], tab[:, 1, :]
        win = sb("win", [P, KD, IN_COLS])
        recb = sb("recb", [P, TB, REC])
        wst = recb[:, :, 0:KD * 512 // 1].rearrange("p t (k n) -> p t k n", k=KD)
        ytmp = sb("ytmp", [P, 12, BT])
        sq = sb("sq", [P, 2, 512])
        rs = sb("rs", [P, 2, 512])
        xt = sb("xt", [P, TB, D])
        hT = sb("hT", [P, 2, KD, BT])
        rowt = sb("rowt", [116, P])
        mod = sb("mod", [P, 2 * KD, 2])
        gain = sb("gain", [P, 2, KD])
        ss = sb("ss", [P, TB])
        rstd = sb("rstd", [P, TB])
        small = sb("small", [P, TB, 48])
        gate = sb("gate", [P, 3, TB, 8])
        dtb = sb("dtb", [P, 8])
        nega = sb("nega", [P, 8])
        eps = sb("eps", [P, 1])
        blrT = sb("blrT", [33, BT])
        w2 = sb("w2", [33, 512])
        PA = [bank(f"acc{i}") for i in range(4)]
        PT = [bank(f"turn{i}") for i in range(2)]
        PL = [bank(f"norm{i}") for i in range(2)]

        tab_in, rows_in, heads_in, small_in, w_in_in = sem("tab_in"), sem("rows_in"), sem("heads_in"), sem("small_in"), {j: sem(f"w_in_in{j}") for j in W_PARTS}
        wmod_in = [sem(f"wmod_in{i}") for i in range(2)]
        x_in, rec_out = sem("x_in"), sem("rec_out")
        cols_full, cols_done, zeroed = sem("cols_full"), sem("cols_done"), sem("zeroed")
        silu_a, silu_v, mod_full, mod_done, nega_a, nega_done = (
            sem("silu_a"), sem("silu_v"), sem("mod_full"), sem("mod_done"), sem("nega_a"), sem("nega_done"))
        job_full, conv_step, conv_done, silu_done = sem("job_full"), sem("conv_step"), sem("conv_done"), sem("silu_done")
        act_evac, narrow_done = sem("act_evac"), sem("narrow_done")
        sq_done, l2_full, l2_ln, rs_done, qk_done = sem("sq_done"), sem("l2_full"), sem("l2_ln"), sem("rs_done"), sem("qk_done")
        turn_full, turn_act, turn_dve = sem("turn_full"), sem("turn_act"), sem("turn_dve")
        ss_done, rstd_ln, rstd_done, xs_done = sem("ss_done"), sem("rstd_ln"), sem("rstd_done"), sem("xs_done")
        gate_a, gate_v, gk_a, gk_ln = sem("gate_a"), sem("gate_v"), sem("gk_a"), sem("gk_ln")
        block = ctx.enter_context(nc.Block())

        x_v = t["x"].rearrange("o (b t p) d -> (o b) p t d", t=TB, p=P)
        c_v = t["ctx"].rearrange("o (t p) d -> (o p) t d", p=P)
        rec_v = rec.rearrange("(b t) p n -> b p t n", t=TB)
        wmod_v = t["w_mod"].rearrange("o (k p) n -> (o p) k n", p=P)
        win_v = t["w_in"].rearrange("o (k p) n -> (o p) k n", p=P)

        def names(last):
            return [n for n in TURNS if not (last and n[0] == "H")]

        def turn_at(b, name, last=False):
            return PT[TURNS.index(name) % 2], 4 + b * NT + names(last).index(name) + 1

        def turn_gone(eng, b, name, last=False):
            act_names = [n for n in names(last) if n in BY_ACT]
            if name in BY_ACT:
                wait(eng, turn_act, 2 + b * NTA + act_names.index(name) + 1)
            else:
                dve_names = [n for n in names(last) if n in BY_DVE]
                wait(eng, turn_dve, 2 + b * NTV + dve_names.index(name) + 1)

        def turn_free(eng, b, name, last=False):
            i = names(last).index(name)
            if i >= 2:
                turn_gone(eng, b, names(last)[i - 2], last)
            elif isinstance(b, int) and b == 0:
                wait(eng, turn_dve if i else turn_act, 2)
            else:
                turn_gone(eng, b - 1, TURNS[NT - 2 + i])

        def job_gone(eng, b, j):
            if j < 6:
                wait(eng, conv_done, b * 6 + j + 1)
            elif j in (10, 11):
                wait(eng, narrow_done, b * 2 + j - 9)
            else:
                wait(eng, act_evac, b * 8 + (j - 5 if j < 10 else j - 7))

        @block.sync
        def _(sp):
            sp.dma_start(tab[:, :, :], t["table"][:, 0:2 * P].rearrange("p (a b) -> p a b", a=2)).then_inc(tab_in, 16)
            sp.dma_start(rowt[0:48, :], t["b_mod"].rearrange("o (r p) -> (o r) p", p=P)).then_inc(rows_in, 16)
            sp.dma_start(rowt[48:56, :], t["attn_norm"].rearrange("o (r p) -> (o r) p", p=P)).then_inc(rows_in, 16)
            sp.dma_start(rowt[56:64, :], t["ffn_norm"].rearrange("o (r p) -> (o r) p", p=P)).then_inc(rows_in, 16)
            sp.dma_start(rowt[64:72, :], t["c"].rearrange("o (r p) -> (o r) p", p=P)).then_inc(rows_in, 16)
            sp.dma_start(rowt[72:80, :], t["c_ctx"].rearrange("(r p) -> r p", p=P)).then_inc(rows_in, 16)
            sp.dma_start(rowt[80:116, :], t["conv_w"].rearrange("o t (r p) -> (o t r) p", p=P)).then_inc(rows_in, 16)
            sp.dma_start(dtb[:, :], t["dt_bias"].rearrange("o d h -> o (d h)").broadcast_to([P, 8])).then_inc(heads_in, 16)
            sp.dma_start(nega[:, :], t["a_log"].rearrange("o d h -> o (d h)").broadcast_to([P, 8])).then_inc(heads_in, 16)
            sp.wait_ge(zeroed, 1)
            for d in range(2):
                sp.dma_start(w2[16 * d:16 * d + 16, 256 * d:256 * d + 256], t["gla_w2"][0, d]).then_inc(small_in, 16)
            sp.dma_start(w2[32:33, :], t["gla_b"].rearrange("o d n -> o (d n)")).then_inc(small_in, 16)
            for g in range(2):
                sp.dma_start(wst[:, g, :, :], wmod_v[:, :, 512 * g:512 * g + 512]).then_inc(wmod_in[g], 16)
            sp.dma_start(xt[:, :, :], c_v).then_inc(x_in, 16)
            for g in range(2, 4):
                sp.wait_ge(mod_full, g - 1)
                sp.dma_start(wst[:, g % 2, :, :], wmod_v[:, :, 512 * g:512 * g + 512]).then_inc(wmod_in[g % 2], 16)
            for j, (c0, c1) in W_PARTS.items():
                sp.dma_start(win[:, :, c0:c1], win_v[:, :, c0:c1]).then_inc(w_in_in[j], 16)

            def load_x(hb):
                wait(sp, turn_full, 4 if isinstance(hb, int) and hb == 1 else 4 + (hb - 2) * NT + 6)
                sp.dma_start(xt[:, :, :], x_v[hb - 1]).then_inc(x_in, 16)

            def store(b, last):
                wait(sp, act_evac, 8 * (b + 1))
                wait(sp, turn_dve, 2 + NTV * (b + 1) - (2 if last else 0))
                sp.dma_start(rec_v[b], recb[:, :, :]).then_inc(rec_out, 16)

            load_x(1)
            store(0, False)
            with sp.Fori(0, 3) as i:
                for u in range(2):
                    load_x(2 * i + u + 2)
                    store(2 * i + u + 1, False)
            load_x(8)
            store(7, False)
            store(8, True)
            sp.wait_ge(rec_out, 16 * NBLK)

        @block.tensor
        def _(pe):
            pe.wait_ge(tab_in, 16)
            pe.wait_ge(rows_in, 96)
            pe.transpose(PT[0][:, 0:116], rowt[:, :], ident[0:116, 0:116]).then_inc(cols_full, 1)
            pe.wait_ge(silu_v, 3)
            for g in range(4):
                pe.wait_ge(wmod_in[g % 2], 16 * (g // 2 + 1))
                for j in range(4):
                    for k in range(KD):
                        mm = pe.matmul(PL[0][:, (4 * g + j) * 2:(4 * g + j) * 2 + 2], wst[:, g % 2, k, j * P:(j + 1) * P],
                                       silu_c[:, :, k], start=k == 0, stop=k == KD - 1)
                mm.then_inc(mod_full, 1)

            def turn_h(hb, b):
                pe.wait_ge(xs_done, hb + 1)
                for g in range(4):
                    if b is None:
                        bank_ = PT[g % 2]
                        if g >= 2:
                            wait(pe, turn_act if g % 2 == 0 else turn_dve, 1)
                    else:
                        bank_, _ = turn_at(b, f"H{g}")
                        turn_free(pe, b, f"H{g}")
                    for j in range(4):
                        k, i = 2 * g + j // 2, j % 2
                        mm = pe.transpose(bank_[:, j * P:(j + 1) * P], xt[:, i, k * P:(k + 1) * P], ident)
                    mm.then_inc(turn_full, 1)

            turn_h(0, None)
            pe.wait_ge(small_in, 16 * 3)

            def main(b, u, ctx_block, last):
                h = hT[:, u, :, :]

                def job(j):
                    job_gone(pe, b if j >= 4 else b - 1, j - 4 if j >= 4 else j + 12)
                    acc = PA[j % 4]
                    if isinstance(b, int) and b == 0 and j in W_PARTS:
                        pe.wait_ge(w_in_in[j], 16)
                    if j < 8:
                        for c in range(2):
                            for k in range(KD):
                                col0 = T_COLS[j] + c * P
                                mm = pe.matmul(acc[:, c * BT:(c + 1) * BT], win[:, k, col0:col0 + P], h[:, k, :],
                                               start=k == 0, stop=k == KD - 1)
                    elif j in (10, 11):
                        i = j - 10
                        for c0, n, o in ((W_BETA, 16, 0), (W_LR, 32, 16)):
                            for k in range(KD):
                                mm = pe.matmul(acc[:, o:o + n], h[:, k, i * P:(i + 1) * P], win[:, k, c0:c0 + n],
                                               start=k == 0, stop=k == KD - 1)
                    else:
                        i, c0, _ = TOK_JOBS[j]
                        for k in range(KD):
                            mm = pe.matmul(acc[:, :], h[:, k, i * P:(i + 1) * P], win[:, k, c0:c0 + 512],
                                           start=k == 0, stop=k == KD - 1)
                    mm.then_inc(job_full, 1)

                def turn(name, sources):
                    bank_, _ = turn_at(b, name, last)
                    turn_free(pe, b, name, last)
                    for s, src in enumerate(sources):
                        mm = pe.transpose(bank_[:, s * P:(s + 1) * P], src, ident)
                    mm.then_inc(turn_full, 1)

                if isinstance(b, int) and b == 0:
                    pe.wait_ge(turn_act, 2)
                    pe.wait_ge(turn_dve, 2)
                else:
                    turn_gone(pe, b - 1, "H2")
                    turn_gone(pe, b - 1, "H3")
                for j in range(8):
                    job(j)
                for i in range(4):
                    pe.wait_ge(sq_done, b * 4 + i + 1)
                    wait(pe, rs_done, b * 4 + i - 1)
                    pe.matmul(PL[i % 2][:, :], ones, sq[:, i % 2, :], start=True, stop=True).then_inc(l2_full, 1)
                for j in (8, 9, 10, 11):
                    job(j)
                pe.wait_ge(silu_done, b * 6 + 6)
                for i in range(2):
                    turn(f"V{i}", [ytmp[:, 8 + h_, i * P:(i + 1) * P] for h_ in range(4)])
                if not last:
                    turn_h(b + 1, b)
                job(12)
                pe.wait_ge(act_evac, b * 8 + 2)
                turn("BK", [recb[:, i, R_BK + c * P:R_BK + (c + 1) * P] for i in range(2) for c in range(2)])
                pe.wait_ge(qk_done, b * 4 + 4)
                for i in range(2):
                    turn(f"K{i}", [recb[:, i, R_KQ + 2 * h_ * P:R_KQ + (2 * h_ + 1) * P] for h_ in range(4)])
                job(13)
                bank_, _ = turn_at(b, "LR")
                turn_free(pe, b, "LR", last)
                pe.wait_ge(narrow_done, b * 2 + 2)
                for i in range(2):
                    mm = pe.transpose(bank_[0:32, i * P:(i + 1) * P], small[:, i, 16:48], ident)
                mm.then_inc(turn_full, 1)
                job(14)
                turn_gone(pe, b, "LR", last)
                for i in range(2):
                    bank_, _ = turn_at(b, f"G{i}")
                    turn_free(pe, b, f"G{i}", last)
                    pe.matmul(bank_[:, :], blrT[:, i * P:(i + 1) * P], w2[:, :], start=True, stop=True).then_inc(turn_full, 1)
                job(15)

            main(0, 0, True, False)
            with pe.Fori(0, 3) as i:
                for u in range(2):
                    main(2 * i + u + 1, (1 + u) % 2, False, False)
            main(7, 1, False, False)
            main(8, 0, False, True)

        @block.scalar
        def _(act):
            nc.scalar.preload_act_table_set("natural_log_exp_and_others")
            act.wait_ge(cols_done, 1)
            act.activation(silu_c[:, :, :], col[:, 64:80].rearrange("p (s k) -> p s k", s=2), ACT.Exp, scale=-1.0).then_inc(silu_a, 1)
            act.wait_ge(heads_in, 32)
            act.activation(nega[:, :], nega[:, :], ACT.Exp).then_inc(nega_a, 1)

            def stats(hb):
                act.wait_ge(x_in, 16 * (hb + 1))
                wait(act, qk_done, 4 * hb)
                wait(act, l2_full, 4 * hb)
                for i in range(TB):
                    if i:
                        act.wait_ge(ss_done, 2 * hb + 1)
                    act.activation(rs[:, :, :].rearrange("p a b -> p (a b)"), xt[:, i, :], ACT.Square,
                                   accum_out=ss[:, i:i + 1]).then_inc(ss_done, 1)
                act.wait_ge(ss_done, 2 * (hb + 1))
                wait(act, xs_done, hb)
                act.activation(rstd[:, :], ss[:, :], ACT.Ln, scale=1.0 / D, bias=eps[:, :]).then_inc(rstd_ln, 1)
                act.wait_ge(rstd_ln, hb + 1)
                act.activation(rstd[:, :], rstd[:, :], ACT.Exp, scale=-0.5).then_inc(rstd_done, 1)

            def evac_h(hb, g, bank_, s):
                for j in range(2):
                    k = 2 * g + j
                    ins = act.activation(hT[:, hb, k, :], bank_[:, j * BT:(j + 1) * BT], ACT.Identity,
                                         scale=gain[:, s, k:k + 1], bias=mod[:, k, s:s + 1])
                ins.then_inc(turn_act, 1)

            act.wait_ge(zeroed, 1)
            stats(0)
            act.wait_ge(mod_done, 3)
            for g in (0, 2):
                act.wait_ge(turn_full, g + 1)
                evac_h(0, g, PT[0], 1)

            def main(b, u, ctx_block, last):
                for j in range(6):
                    act.wait_ge(conv_done, b * 6 + j + 1)
                    y = ytmp[:, 2 * j:2 * j + 2, :]
                    act.activation(y, y, ACT.Silu).then_inc(silu_done, 1)
                act.preload_act_table_set("natural_log_exp_and_others")
                wait(act, rec_out, 16 * b)

                def to_rec(j):
                    act.wait_ge(job_full, b * 16 + j + 1)
                    if j < 8:
                        o = R_BQ if j == 6 else R_BK
                        dst = recb[:, :, o:o + 2 * P].rearrange("p t (c n) -> p c t n", c=2)
                        src = PA[j % 4][:, :].rearrange("p (c t n) -> p c t n", c=2, t=TB)
                        act.activation(dst, src, ACT.Copy, scale=0.125 if j == 6 else 1.0).then_inc(act_evac, 1)
                    else:
                        i, _, o = TOK_JOBS[j]
                        act.activation(recb[:, i, o:o + 512], PA[j % 4][:, :], ACT.Copy).then_inc(act_evac, 1)

                to_rec(6)
                to_rec(7)
                for i in range(4):
                    act.wait_ge(l2_full, b * 4 + i + 1)
                    wait(act, qk_done, b * 4 + i - 1)
                    act.activation(rs[:, i % 2, :], PL[i % 2][:, :], ACT.Ln, bias=eps[:, :]).then_inc(l2_ln, 1)
                    act.wait_ge(l2_ln, b * 4 + i + 1)
                    act.activation(rs[:, i % 2, :], rs[:, i % 2, :], ACT.Exp, scale=-0.5).then_inc(rs_done, 1)
                to_rec(8)
                to_rec(9)
                if not last:
                    stats(b + 1)

                def turned(name, dst):
                    bank_, full = turn_at(b, name, last)
                    act.wait_ge(turn_full, full)
                    act.activation(dst, bank_[:, :], ACT.Copy).then_inc(turn_act, 1)

                turned("V0", recb[:, 0, R_V:R_V + 512])
                if not last:
                    for g in (0, 2):
                        bank_, full = turn_at(b, f"H{g}")
                        act.wait_ge(turn_full, full)
                        evac_h(1 - u, g, bank_, 0)
                to_rec(12)
                bank_, full = turn_at(b, "BK", last)
                act.wait_ge(turn_full, full)
                act.activation(recb[:, :, R_BKTOK:R_BKTOK + 256], bank_[:, :].rearrange("p (t n) -> p t n", t=2), ACT.Copy).then_inc(turn_act, 1)
                act.wait_ge(narrow_done, b * 2 + 2)
                wait(act, gate_v, b * 6 + 1)
                act.activation(gate[:, 0, :, :], small[:, :, 0:8], ACT.Exp, scale=-1.0).then_inc(gate_a, 1)
                act.activation(gate[:, 2, :, :], gate[:, 1, :, :], ACT.Abs).then_inc(gate_a, 1)
                act.wait_ge(gate_a, b * 4 + 2)
                act.activation(gate[:, 2, :, :], gate[:, 2, :, :], ACT.Exp, scale=-1.0).then_inc(gate_a, 1)
                act.wait_ge(gate_a, b * 4 + 3)
                act.activation(gate[:, 2, :, :], gate[:, 2, :, :], ACT.Ln, bias=1.0).then_inc(gate_a, 1)
                bank_, full = turn_at(b, "K1", last)
                act.wait_ge(turn_full, full)
                act.activation(recb[:, 1, R_KTOK:R_KTOK + 512], bank_[:, :], ACT.Copy).then_inc(turn_act, 1)
                to_rec(13)
                to_rec(14)
                for i in range(2):
                    bank_, full = turn_at(b, f"G{i}", last)
                    act.wait_ge(turn_full, full)
                    if i == 0:
                        wait(act, qk_done, b * 4 + 4)
                    act.activation(rs[:, i, :], bank_[:, :], ACT.Abs).then_inc(gk_ln, 1)
                    act.wait_ge(gk_ln, b * 4 + 2 * i + 1)
                    act.activation(rs[:, i, :], rs[:, i, :], ACT.Exp, scale=-1.0).then_inc(gk_ln, 1)
                    act.wait_ge(gk_ln, b * 4 + 2 * i + 2)
                    act.activation(rs[:, i, :], rs[:, i, :], ACT.Ln, bias=1.0).then_inc(gk_a, 1)
                to_rec(15)

            main(0, 0, True, False)
            with act.Fori(0, 3) as i:
                for u in range(2):
                    main(2 * i + u + 1, (1 + u) % 2, False, False)
            main(7, 1, False, False)
            main(8, 0, False, True)

        @block.vector
        def _(dve):
            dve.memset(w2[:, :], 0.0)
            dve.memset(blrT[32:33, :], 1.0)
            dve.memset(eps[:, :], EPS).then_inc(zeroed, 1)
            dve.wait_ge(cols_full, 1)
            dve.tensor_copy(col[:, :], PT[0][:, 0:116]).then_inc(cols_done, 1)
            dve.wait_ge(silu_a, 1)
            dve.tensor_scalar(silu_c[:, :, :], silu_c[:, :, :], 1.0, None, ALU.add).then_inc(silu_v, 1)
            dve.wait_ge(silu_v, 1)
            dve.reciprocal(silu_c[:, :, :], silu_c[:, :, :]).then_inc(silu_v, 1)
            dve.wait_ge(silu_v, 2)
            dve.wait_ge(cols_done, 1)
            dve.tensor_tensor(silu_c[:, :, :], silu_c[:, :, :], col[:, 64:80].rearrange("p (s k) -> p s k", s=2), ALU.mult).then_inc(silu_v, 1)
            dve.wait_ge(nega_a, 1)
            dve.tensor_scalar(nega[:, :], nega[:, :], -1.0, None, ALU.mult).then_inc(nega_done, 1)
            dve.wait_ge(mod_full, 4)
            dve.tensor_tensor(mod[:, :, :], PL[0][:, 0:4 * KD].rearrange("p (c s) -> p c s", s=2), lanes(col[:, 0:2 * KD], 2), ALU.add).then_inc(mod_done, 1)
            dve.wait_ge(mod_done, 1)
            for s in range(2):
                dve.scalar_tensor_tensor(out=gain[:, s, :], in0=mod[:, KD:2 * KD, s], scalar=1.0, in1=col[:, 48:56], op0=ALU.add, op1=ALU.mult).then_inc(mod_done, 1)

            def scale_x(hb):
                dve.wait_ge(rstd_done, hb + 1)
                for i in range(TB):
                    ins = dve.tensor_scalar(xt[:, i, :], xt[:, i, :], rstd[:, i:i + 1], None, ALU.mult)
                ins.then_inc(xs_done, 1)

            def evac_h(hb, g, bank_, s):
                for j in range(2):
                    k = 2 * g + j
                    ins = dve.tensor_scalar(hT[:, hb, k, :], bank_[:, j * BT:(j + 1) * BT], gain[:, s, k:k + 1],
                                            mod[:, k, s:s + 1], ALU.mult, ALU.add)
                ins.then_inc(turn_dve, 1)

            dve.wait_ge(mod_done, 3)
            scale_x(0)
            for g in (1, 3):
                dve.wait_ge(turn_full, g + 1)
                evac_h(0, g, PT[1], 1)

            def main(b, u, ctx_block, last):
                n_rows, width = (1, BT) if ctx_block else (BT // GRID_W, GRID_W)
                for j in range(6):
                    dve.wait_ge(job_full, b * 16 + j + 1)
                    if j == 0:
                        wait(dve, sq_done, b * 4)
                    if j == 4:
                        bank_, full = turn_at(b - 1, "V1")
                        if not (isinstance(b, int) and b == 0):
                            wait(dve, turn_full, full)
                    for tap in (1, 0, 2):
                        for c in range(2):
                            ch = 2 * j + c
                            w = col[:, 80 + tap * 12 + ch:80 + tap * 12 + ch + 1]
                            u_ = PA[j % 4][:, c * BT:(c + 1) * BT].rearrange("p (r w) -> p r w", r=n_rows)
                            y = ytmp[:, ch, :].rearrange("p (r w) -> p r w", r=n_rows)
                            if tap == 1:
                                ins = dve.tensor_scalar(y, u_, w, None, ALU.mult)
                            elif tap == 0:
                                ins = dve.scalar_tensor_tensor(out=y[:, :, 1:width], in0=u_[:, :, 0:width - 1], scalar=w,
                                                               in1=y[:, :, 1:width], op0=ALU.mult, op1=ALU.add)
                            else:
                                ins = dve.scalar_tensor_tensor(out=y[:, :, 0:width - 1], in0=u_[:, :, 1:width], scalar=w,
                                                               in1=y[:, :, 0:width - 1], op0=ALU.mult, op1=ALU.add)
                        if tap == 2:
                            ins.then_inc(conv_done, 1)
                        else:
                            ins.then_inc(conv_step, 1)
                            dve.wait_ge(conv_step, b * 12 + 2 * j + (1 if tap == 1 else 2))
                wait(dve, rec_out, 16 * b)
                for i in range(4):
                    dve.wait_ge(rs_done, b * 4 + i + 1)
                    for c in range(2):
                        h_ = 2 * (i % 2) + c
                        o = R_KQ + (2 * h_ + (1 if i < 2 else 0)) * P
                        ins = dve.scalar_tensor_tensor(out=recb[:, :, o:o + P], in0=ytmp[:, 2 * i + c, :].rearrange("p (t n) -> p t n", t=2),
                                                       scalar=P ** -0.5 if i < 2 else 1.0,
                                                       in1=rs[:, i % 2, c * BT:(c + 1) * BT].rearrange("p (t n) -> p t n", t=2),
                                                       op0=ALU.mult, op1=ALU.mult)
                    ins.then_inc(qk_done, 1)
                for i in range(2):
                    dve.wait_ge(job_full, b * 16 + 11 + i)
                    if i == 0 and not (isinstance(b, int) and b == 0):
                        _, full = turn_at(b - 1, "LR")
                        dve.wait_ge(turn_full, full)
                    dve.tensor_copy(small[:, i, :], PA[(10 + i) % 4][:, 0:48]).then_inc(narrow_done, 1)
                if not last:
                    scale_x(b + 1)
                bank_, full = turn_at(b, "V1", last)
                dve.wait_ge(turn_full, full)
                dve.tensor_copy(recb[:, 1, R_V:R_V + 512], bank_[:, :]).then_inc(turn_dve, 1)
                if not last:
                    for g in (1, 3):
                        bank_, full = turn_at(b, f"H{g}")
                        dve.wait_ge(turn_full, full)
                        evac_h(1 - u, g, bank_, 0)
                dve.wait_ge(narrow_done, b * 2 + 2)
                wait(dve, gate_a, b * 4)
                dve.tensor_tensor(gate[:, 1, :, :], small[:, :, 8:16], rows(dtb[:, :], 2), ALU.add).then_inc(gate_v, 1)
                bank_, full = turn_at(b, "K0", last)
                dve.wait_ge(turn_full, full)
                dve.tensor_copy(recb[:, 0, R_KTOK:R_KTOK + 512], bank_[:, :]).then_inc(turn_dve, 1)
                dve.wait_ge(gate_a, b * 4 + 1)
                dve.tensor_scalar(gate[:, 0, :, :], gate[:, 0, :, :], 1.0, None, ALU.add).then_inc(gate_v, 1)
                dve.wait_ge(gate_v, b * 6 + 2)
                dve.reciprocal(gate[:, 0, :, :], gate[:, 0, :, :]).then_inc(gate_v, 1)
                dve.wait_ge(gate_v, b * 6 + 3)
                dve.tensor_scalar(recb[:, :, R_NB:R_NB + 8], gate[:, 0, :, :], -1.0, None, ALU.mult).then_inc(gate_v, 1)
                dve.wait_ge(gate_a, b * 4 + 4)
                dve.scalar_tensor_tensor(out=gate[:, 1, :, :], in0=gate[:, 1, :, :], scalar=0.0, in1=gate[:, 2, :, :], op0=ALU.max, op1=ALU.add).then_inc(gate_v, 1)
                dve.wait_ge(gate_v, b * 6 + 5)
                dve.tensor_tensor(recb[:, :, R_G:R_G + 8], gate[:, 1, :, :], rows(nega[:, :], 2), ALU.mult).then_inc(gate_v, 1)
                bank_, full = turn_at(b, "LR", last)
                dve.wait_ge(turn_full, full)
                dve.tensor_copy(blrT[0:32, :], bank_[0:32, 0:BT]).then_inc(turn_dve, 1)
                for i in range(2):
                    bank_, _ = turn_at(b, f"G{i}")
                    dve.wait_ge(gk_a, b * 2 + i + 1)
                    dve.scalar_tensor_tensor(out=recb[:, i, R_GK:R_GK + 512], in0=bank_[:, :], scalar=0.0, in1=rs[:, i, :],
                                             op0=ALU.min, op1=ALU.subtract).then_inc(turn_dve, 1)

            main(0, 0, True, False)
            with dve.Fori(0, 3) as i:
                for u in range(2):
                    main(2 * i + u + 1, (1 + u) % 2, False, False)
            main(7, 1, False, False)
            main(8, 0, False, True)

        @block.gpsimd
        def _(pool):
            def main(b):
                for i in range(4):
                    pool.wait_ge(silu_done, b * 6 + i + 1)
                    wait(pool, l2_full, b * 4 + i - 1)
                    y = ytmp[:, 2 * i:2 * i + 2, :].rearrange("p a b -> p (a b)")
                    pool.tensor_tensor(sq[:, i % 2, :], y, y, ALU.mult).then_inc(sq_done, 1)

            main(0)
            with pool.Fori(1, NBLK) as b:
                main(b)


MODC = 4 * D // (CHUNKS - CHUNKS_CTX)
MOD_STEPS = 4


def stage_mixers(nc, t, rec, mixed, silu_c, mod_sums):
    steps_ctx, lat = CHUNKS_CTX, CHUNKS - CHUNKS_CTX
    dirs = (0, 1)
    with ExitStack() as ctx:
        sb = lambda name, shape, dt=F32: ctx.enter_context(nc.sbuf_tensor(name, shape, dt))
        two = lambda name, shape: [sb(f"{name}{d}", shape) for d in dirs]
        sem, clear = semaphores(nc)
        ctx.callback(clear)
        pair = lambda name: [sem(f"{name}_{s}") for s in ("fwd", "bwd")]
        tab = sb("tab3", [P, NTAB, P])
        masks = sb("masks3", [P, 2, NMASK, P], I8)
        ident = tab[:, C_ID, :]
        rin = [[sb(f"rin{d}{u}", [P, MIX]) for u in range(2)] for d in dirs]
        gsm, esm = two("gsm", [P, 12]), two("esm", [P, 12])
        decay = two("decay", [P, HA, P])
        resid = decay
        sysT = two("sysT", [P, HA, P])
        o_inter = sysT
        qkd = two("qkd", [P, HA, P])
        first_y = two("first_y", [P, HA, P])
        steps_t = [[sb(f"step{d}{l}", [P, HA, P]) for l in range(NLEV + 1)] for d in dirs]
        inv, invT = two("inv", [P, HA, P]), two("invT", [P, HA, P])
        v_dec = inv
        v_new = two("v_new", [P, HA, P])
        state_a = two("state_a", [P, HA, P])
        ex, exb, exm = two("ex", [P, 2, 4, P]), two("exb", [P, 512]), two("exm", [P, 256])
        ql, kl = two("ql", [P, 2, 2, 5, P]), two("kl", [P, 2, 4, P])
        k_dec, score = two("k_dec", [P, 256]), two("score", [P, HA, P])
        state_b = two("state_b", [P, 2, P])
        outb = two("outb", [P, 1024])
        wst, mod_acc = sb("wst3", [P, KD, MODC]), sb("mod_acc", [P, MODC])
        BT_, BX, BY, BB = ([ctx.enter_context(nc.psum_tensor(f"{n}{d}", [P, 512], F32)) for d in dirs]
                           for n in ("bank_t", "bank_x", "bank_y", "bank_b"))
        by_head = lambda bank: bank[:, :].rearrange("p (h n) -> p h n", h=HA)

        tab_in, masks_in, masks_done, init_done = sem("tab_in3"), sem("masks_in3"), sem("masks_done"), sem("init_done")
        rec_in = [[sem(f"rec_in{d}{u}") for u in range(2)] for d in dirs]
        gc_full, gc_out, gr_full, dd_done, ddm_done, gl_done, esm_done, decay_done = map(
            pair, ("gc_full", "gc_out", "gr_full", "dd_done", "ddm_done", "gl_done", "esm_done", "decay_done"))
        kq_full, sys_done, qkd_done, sys_turned, first_done = map(pair, ("kq_full", "sys_done", "qkd_done", "sys_turned", "first_done"))
        t_full, t_done, x_full, x_out, y_full, y_out = map(pair, ("t_full", "t_done", "x_full", "x_out", "y_full", "y_out"))
        ks_full, r_done, qs_full, qs_out, z_full, vn_done, vd_done, oi_full, oa_done, su_full, s_done = map(
            pair, ("ks_full", "r_done", "qs_full", "qs_out", "z_full", "vn_done", "vd_done", "oi_full", "oa_done", "su_full", "s_done"))
        ex_full, ex_done, ql_done, kl_done, sc_full, sc_done, ob_full, ob_done, sub_full, bs_done, out_st = map(
            pair, ("ex_full", "ex_done", "ql_done", "kl_done", "sc_full", "sc_done", "ob_full", "ob_done", "sub_full", "bs_done", "out_st"))
        wmod_in, mod_step, mod_st = sem("wmod_in3"), sem("mod_step"), sem("mod_st")
        block = ctx.enter_context(nc.Block())
        wmod_v = t["w_mod"].rearrange("o (k p) n -> (o p) k n", p=P)

        both = lambda f, *a: [f(d, *a) for d in dirs]
        last = (P - 1, 0)
        const = lambda c, d: tab[:, c + d, :]
        w_cols = lambda d, a, b: tab[:, C_W + 5 * d + a:C_W + 5 * d + b, :].rearrange("p a b -> p (a b)")
        mask4 = lambda d, m: rows(masks[:, d, m, :], HA)

        def scale_q(eng, d, u):
            for h in range(2):
                r = slice(64 * h, 64 * h + 64)
                for p in range(2):
                    eng.tensor_tensor(ql[d][r, p, h, 0:4, :], rows(rin[d][u][r, R_BQ + p * P:R_BQ + (p + 1) * P], 4), ex[d][r, p, :, :], ALU.mult)
                ins = eng.tensor_tensor(ql[d][r, :, h, 4, :], rin[d][u][r, R_BQ:R_BQ + 256].rearrange("p (a b) -> p a b", a=2),
                                        exb[d][r, 0:256].rearrange("p (a b) -> p a b", a=2), ALU.mult)
            return ins

        @block.sync
        def _(sp):
            sp.dma_start(tab[:, :, :], t["table"].rearrange("p (a b) -> p a b", b=P)).then_inc(tab_in, 16)
            sp.dma_start(rin[1][1][:, 0:2 * NMASK * P], t["masks"]).then_inc(masks_in, 16)

            def load(d, n, u, chunk):
                sp.dma_start(rin[d][u][:, :], rec[chunk, :, 0:MIX]).then_inc(rec_in[d][u], 16)

            def store(d, n, chunks):
                chunk = chunks[d]
                sp.wait_ge(masks_in, 16)
                wait(sp, oa_done[d], n - 1)
                wait(sp, ob_done[d], n - 1)
                sp.dma_start(mixed[d, chunk], outb[d][:, :]).then_inc(out_st[d], 16)

            def load_next(d, n, u, chunks):
                sp.wait_ge(masks_in, 16)
                wait(sp, su_full[d], n + 1)
                wait(sp, sub_full[d], n + 1)
                load(d, n + 2, u, chunks[d])

            for n in range(2):
                if n == 1:
                    sp.wait_ge(masks_done, 1)
                load(0, n, n, n)
                load(1, n, n, steps_ctx - 1 - n)
            def load_mod(n, at):
                sp.wait_ge(masks_in, 16)
                wait(sp, mod_step, MOD_STEPS * (n - 2))
                sp.dma_start(wst[:, :, :], at).then_inc(wmod_in, 16)

            def store_mod(n):
                sp.wait_ge(masks_in, 16)
                wait(sp, mod_step, MOD_STEPS * (n - 1))
                sp.dma_start(mod_sums[n - 2], mod_acc[:, :]).then_inc(mod_st, 16)

            load_mod(2, wmod_v[:, :, 2 * D:2 * D + MODC])
            for n in range(2):
                both(load_next, n, n, (n + 2, CHUNKS - 1 - n))
            with sp.Fori(1, CHUNKS // 2 - 1) as i:
                for u in range(2):
                    n = 2 * i + u
                    both(store, n, (n - 2, CHUNKS - 1 - n))
                    both(load_next, n, u, (n + 2, CHUNKS - 1 - n))
                    store_mod(n)
                    load_mod(n + 1, wmod_v[:, :, bass.ds(2 * D + MODC * (n - 1), MODC)])
            for n in (CHUNKS - 2, CHUNKS - 1):
                both(store, n, (n - 2, CHUNKS - 1 - n))
                store_mod(n)
                if n < CHUNKS - 1:
                    load_mod(n + 1, wmod_v[:, :, 2 * D + MODC * (n - 1):2 * D + MODC * n])
            sp.wait_ge(mod_st, 16 * lat)
            for d in dirs:
                sp.wait_ge(out_st[d], 16 * lat)

        @block.tensor
        def _(pe):
            pe.wait_ge(tab_in, 16)

            def four(bank, lhs, rhs):
                for h in range(HA):
                    mm = pe.matmul(bank[:, h * P:(h + 1) * P], lhs(h), rhs(h), start=True, stop=True)
                return mm

            def gates(d, n, u, i):
                g = rin[d][u][:, R_G + 4 * d:R_G + 4 * d + 4]
                pe.wait_ge(rec_in[d][u], 16 * (i + 1))
                pe.wait_ge(s_done[d], n + 1)
                pe.matmul(BY[d][:, 0:4], const(C_TRI, d), g, start=True, stop=True).then_inc(gc_full[d], 1)
                wait(pe, vn_done[d], n)
                four(BT_[d], lambda h: g[:, h:h + 1].broadcast_to([P, P]), lambda h: const(C_TRI, d)).then_inc(gr_full[d], 1)

            def exponents(d, n, u, p):
                gk = rin[d][u][:, R_GK + 256 * d:R_GK + 256 * d + 256]
                if p == 0:
                    pe.wait_ge(bs_done[d], n + 1)
                else:
                    pe.wait_ge(ex_done[d], 3 * n + p)
                if p < 2:
                    mm = pe.matmul(BB[d][:, :], gk[:, p * P:(p + 1) * P], w_cols(d, 0, 4), start=True, stop=True)
                else:
                    for q in range(2):
                        pe.matmul(BB[d][:, q * P:(q + 1) * P], gk[:, q * P:(q + 1) * P], w_cols(d, 4, 5), start=True, stop=True)
                    mm = pe.matmul(BB[d][:, 256:512], const(C_SUF, d), gk, start=True, stop=True)
                mm.then_inc(ex_full[d], 1)

            def products(d, n, u):
                wait(pe, r_done[d], n)
                wait(pe, oa_done[d], n - 2)
                pe.wait_ge(gc_out[d], n + 1)
                for h in range(HA):
                    kq = rin[d][u][:, R_KQ + 2 * h * P:R_KQ + 2 * (h + 1) * P]
                    bank = BX[d] if h < 2 else BY[d]
                    mm = pe.matmul(bank[:, (h % 2) * 256:(h % 2) * 256 + 256], kq[:, 0:P], kq, start=True, stop=True)
                mm.then_inc(kq_full[d], 1)

            def turn(d, n):
                pe.wait_ge(sys_done[d], n + 1)
                pe.wait_ge(gl_done[d], n + 1)
                for h in range(HA):
                    mm = pe.transpose(BT_[d][:, h * P:(h + 1) * P], sysT[d][:, h, :], ident)
                mm.then_inc(sys_turned[d], 1)

            def level_t(d, n, l):
                x = steps_t[d][0] if l == 0 else inv[d]
                if l == 0:
                    pe.wait_ge(first_done[d], 2 * n + 2)
                else:
                    pe.wait_ge(x_out[d], 5 * n + l)
                four(BT_[d], lambda h: sysT[d][:, h, :], lambda h: x[:, h, :]).then_inc(t_full[d], 1)

            def level_xy(d, n, l):
                y = first_y[d] if l == 0 else invT[d]
                step = steps_t[d][l + 1]
                pe.wait_ge(t_done[d], NLEV * n + l + 1)
                if l == 0:
                    pe.wait_ge(qkd_done[d], n + 1)
                else:
                    pe.wait_ge(y_out[d], NLEV * n + l)
                if l < NLEV - 1:
                    four(BX[d], lambda h: y[:, h, :], lambda h: step[:, h, :]).then_inc(x_full[d], 1)
                four(BY[d], lambda h: step[:, h, :], lambda h: y[:, h, :]).then_inc(y_full[d], 1)

            def scores(d, n, v):
                if v == 0:
                    pe.wait_ge(ex_done[d], 3 * n + 3)
                    pe.wait_ge(ql_done[d], n + 1)
                    pe.wait_ge(kl_done[d], n + 1)
                else:
                    pe.wait_ge(sc_done[d], 4 * n + v)
                for p in range(2):
                    mm = pe.matmul(BB[d][:, p * 256:(p + 1) * 256], kl[d][:, p, v, :], ql[d][:, p, :, v + 1, :], start=True, stop=True)
                mm.then_inc(sc_full[d], 1)

            def out_b(d, n, u):
                bv = rin[d][u][:, R_BV:R_BV + 512]
                pe.wait_ge(sc_done[d], 4 * n + 4)
                for h in range(HA):
                    pe.matmul(BB[d][:, h * P:(h + 1) * P], score[d][:, h, :], bv[:, h * P:(h + 1) * P], start=True, stop=False)
                    mm = pe.matmul(BB[d][:, h * P:(h + 1) * P], ql[d][:, h // 2, h % 2, 0, :], state_b[d][:, h // 2, :], start=False, stop=True)
                mm.then_inc(ob_full[d], 1)

            def update_b(d, n, u, ctx_step):
                if ctx_step:
                    pe.wait_ge(sc_done[d], 4 * n + 4)
                else:
                    pe.wait_ge(ob_done[d], n - 1)
                for p in range(2):
                    mm = pe.matmul(BB[d][:, p * 256:(p + 1) * 256], k_dec[d][:, p * P:(p + 1) * P],
                                   rin[d][u][:, R_BV + 256 * p:R_BV + 256 * p + 256], start=True, stop=True)
                mm.then_inc(sub_full[d], 1)

            kT = lambda d, u, h: rin[d][u][:, R_KQ + 2 * h * P:R_KQ + (2 * h + 1) * P]
            qT = lambda d, u, h: rin[d][u][:, R_KQ + (2 * h + 1) * P:R_KQ + (2 * h + 2) * P]

            def state_k(d, n, u):
                pe.wait_ge(x_out[d], 5 * n + 5)
                four(BX[d], lambda h: kT(d, u, h), lambda h: state_a[d][:, h, :]).then_inc(ks_full[d], 1)

            def state_q(d, n, u):
                pe.wait_ge(r_done[d], n + 1)
                four(BX[d], lambda h: qT(d, u, h), lambda h: state_a[d][:, h, :]).then_inc(qs_full[d], 1)

            def solve(d, n):
                pe.wait_ge(r_done[d], n + 1)
                pe.wait_ge(y_out[d], NLEV * (n + 1))
                four(BT_[d], lambda h: invT[d][:, h, :], lambda h: resid[d][:, h, :]).then_inc(z_full[d], 1)

            def out_a(d, n):
                pe.wait_ge(vn_done[d], n + 1)
                pe.wait_ge(qs_out[d], n - 1)
                four(BX[d], lambda h: qkd[d][:, h, :], lambda h: v_new[d][:, h, :]).then_inc(oi_full[d], 1)

            def update_a(d, n, u):
                pe.wait_ge(vd_done[d], n + 1)
                four(BY[d], lambda h: rin[d][u][:, R_KTOK + h * P:R_KTOK + (h + 1) * P],
                     lambda h: v_dec[d][:, h, :]).then_inc(su_full[d], 1)

            def step(n, u, i, ctx_step):
                both(gates, n, u, i)
                both(exponents, n, u, 0)
                both(products, n, u)
                both(exponents, n, u, 1)
                both(turn, n)
                both(exponents, n, u, 2)
                for l in range(NLEV - 1):
                    both(level_t, n, l)
                    both(level_xy, n, l)
                    if l >= 1:
                        both(scores, n, l - 1)
                both(level_t, n, NLEV - 1)
                both(state_k, n, u)
                both(level_xy, n, NLEV - 1)
                if not ctx_step:
                    both(state_q, n, u)
                both(solve, n)
                if not ctx_step:
                    both(out_b, n, u)
                    both(out_a, n)
                both(update_b, n, u, ctx_step)
                both(update_a, n, u)

            for n in range(2):
                step(n, n, 0, True)
            with pe.Fori(1, CHUNKS // 2) as i:
                for u in range(2):
                    step(2 * i + u, u, i, False)

        @block.scalar
        def _(act):
            act.preload_act_table_set("natural_log_exp_and_others")

            def decays(d, n):
                act.wait_ge(gl_done[d], n + 1)
                act.wait_ge(s_done[d], n + 1)
                wait(act, vd_done[d], n)
                act.activation(esm[d][:, :], gsm[d][:, :], ACT.Exp).then_inc(esm_done[d], 1)
                act.wait_ge(ddm_done[d], n + 1)
                act.activation(decay[d][:, :, :], decay[d][:, :, :], ACT.Exp).then_inc(decay_done[d], 1)

            def exponentials(d, n, p):
                act.wait_ge(ex_full[d], 3 * n + p + 1)
                if p == 0:
                    wait(act, ql_done[d], n)
                    wait(act, kl_done[d], n)
                if p < 2:
                    act.activation(ex[d][:, p, :, :].rearrange("p a b -> p (a b)"), BB[d][:, :], ACT.Exp, scale=1 / NORMALIZER).then_inc(ex_done[d], 1)
                else:
                    act.activation(exm[d][:, :], BB[d][:, 0:256], ACT.Exp, scale=-1 / NORMALIZER)
                    act.activation(exb[d][:, :], BB[d][:, :], ACT.Exp, scale=1 / NORMALIZER).then_inc(ex_done[d], 1)

            def inverse_x(d, n, l):
                act.wait_ge(x_full[d], 5 * n + l + 1)
                act.activation(inv[d][:, :, :], by_head(BX[d]), ACT.Copy).then_inc(x_out[d], 1)

            def inverse_y(d, n, l):
                act.wait_ge(y_full[d], NLEV * n + l + 1)
                act.activation(invT[d][:, :, :], by_head(BY[d]), ACT.Copy).then_inc(y_out[d], 1)

            def copy_b(d, n):
                act.wait_ge(ob_full[d], n - 1)
                wait(act, out_st[d], 16 * (n - 2))
                act.activation(outb[d][:, 512:1024], BB[d][:, :], ACT.Copy).then_inc(ob_done[d], 1)

            def decay_q(d, n):
                act.wait_ge(qs_full[d], n - 1)
                act.wait_ge(esm_done[d], n + 1)
                for h in range(HA):
                    ins = act.activation(o_inter[d][:, h, :], BX[d][:, h * P:(h + 1) * P], ACT.Copy, scale=esm[d][:, h:h + 1])
                ins.then_inc(qs_out[d], 1)

            def step(n, u, ctx_step):
                both(decays, n)
                for p in range(3):
                    both(exponentials, n, p)
                for l in range(NLEV - 1):
                    for d in dirs:
                        inverse_x(d, n, l)
                        inverse_y(d, n, l)
                both(inverse_y, n, NLEV - 1)
                if not ctx_step:
                    both(decay_q, n)
                    both(copy_b, n)

            for n in range(2):
                step(n, n, True)
            with act.Fori(1, CHUNKS // 2) as i:
                for u in range(2):
                    step(2 * i + u, u, False)

        @block.vector
        def _(dve):
            for d in dirs:
                dve.memset(state_a[d][:, :, :], 0.0).then_inc(s_done[d], 1)
                dve.memset(state_b[d][:, :, :], 0.0).then_inc(bs_done[d], 1)
                dve.memset(score[d][:, :, :], 0.0)
            dve.memset(ql[1][:, :, :, :, :], 0.0)
            dve.wait_ge(tab_in, 16)
            for d in dirs:
                for x in (first_y[d], *steps_t[d]):
                    ins = dve.tensor_copy(x[:, :, :], rows(ident, HA))
            ins.then_inc(init_done, 1)
            dve.wait_ge(init_done, 1)
            dve.wait_ge(masks_in, 16)
            dve.tensor_copy(masks[:, :, :, :].rearrange("p d a b -> p (d a b)"), rin[1][1][:, 0:2 * NMASK * P]).then_inc(masks_done, 1)
            dve.wait_ge(masks_done, 1)

            def wait_apart(*pairs):
                values = [v if isinstance(v, int) else dve.to_reg(v) for v in pairs[1::2]]
                dve.wait_ge(tab_in, 16)
                for sem_, v in zip(pairs[::2], values):
                    wait(dve, sem_, v)

            def sums(d, n):
                g = gsm[d]
                dve.wait_ge(gc_full[d], n + 1)
                wait(dve, esm_done[d], n)
                dve.tensor_copy(g[:, 0:4], BY[d][:, 0:4]).then_inc(gc_out[d], 1)
                dve.wait_ge(gr_full[d], n + 1)
                dve.wait_ge(gc_out[d], n + 1)
                dve.tensor_tensor(decay[d][:, :, :], by_head(BT_[d]), lanes(g[:, 0:4], P), ALU.subtract).then_inc(dd_done[d], 1)
                dve.tensor_copy(g[:, 4:8], by_head(BT_[d])[:, :, last[d]])
                dve.tensor_tensor(g[:, 8:12], by_head(BT_[d])[:, :, last[d]], g[:, 0:4], ALU.subtract).then_inc(gl_done[d], 1)

            def system(d, n, u):
                nb = rin[d][u][:, R_NB + 4 * d:R_NB + 4 * d + 4]
                dve.wait_ge(kq_full[d], n + 1)
                dve.wait_ge(decay_done[d], n + 1)
                for h in range(HA):
                    kk = (BX, BY)[h // 2][d][:, (h % 2) * 256:(h % 2) * 256 + P]
                    ins = dve.scalar_tensor_tensor(out=sysT[d][:, h, :], in0=kk, scalar=nb[:, h:h + 1], in1=decay[d][:, h, :],
                                                   op0=ALU.mult, op1=ALU.mult)
                ins.then_inc(sys_done[d], 1)
                wait(dve, qkd_done[d], n)
                for j, bank in enumerate((BX[d], BY[d])):
                    kq = bank[:, :].rearrange("p (h a n) -> p h a n", h=2, a=2)[:, :, 1, :]
                    ins = dve.tensor_tensor(qkd[d][:, 2 * j:2 * j + 2, :], kq, decay[d][:, 2 * j:2 * j + 2, :], ALU.mult)
                ins.then_inc(qkd_done[d], 1)

            def first(d, n):
                wait_apart(sys_done[d], n + 1)
                dve.copy_predicated(first_y[d][:, :, :], mask4(d, M_FIRST_T), sysT[d][:, :, :]).then_inc(first_done[d], 1)
                wait_apart(sys_turned[d], n + 1)
                dve.copy_predicated(steps_t[d][0][:, :, :], mask4(d, M_LEV), by_head(BT_[d])).then_inc(first_done[d], 1)

            def decayed_k(d, n, u):
                bk = rin[d][u][:, R_BK:R_BK + 256]
                dve.wait_ge(ex_done[d], 3 * n + 3)
                for p in range(2):
                    dve.tensor_tensor(kl[d][:, p, 0:3, :], rows(bk[:, p * P:(p + 1) * P], 3), ex[d][:, p, 1:4, :], ALU.mult)
                dve.tensor_tensor(kl[d][:, :, 3, :], bk.rearrange("p (a b) -> p a b", a=2),
                                  exm[d][:, :].rearrange("p (a b) -> p a b", a=2), ALU.mult)
                dve.tensor_tensor(k_dec[d][:, :], rin[d][u][:, R_BKTOK:R_BKTOK + 256], exb[d][:, 256:512], ALU.mult).then_inc(kl_done[d], 1)

            def decayed_q(n, u):
                dve.wait_ge(ex_done[1], 3 * n + 3)
                wait(dve, sub_full[1], n)
                scale_q(dve, 1, u).then_inc(ql_done[1], 1)

            def level(d, n, l):
                wait_apart(t_full[d], NLEV * n + l + 1)
                dve.copy_predicated(steps_t[d][l + 1][:, :, :], mask4(d, M_LEV + l + 1), by_head(BT_[d])).then_inc(t_done[d], 1)

            def mask_scores(d, n, v):
                wait_apart(sc_full[d], 4 * n + v + 1, sc_done[d], 4 * n + v)
                dve.copy_predicated(score[d][:, :, :], mask4(d, M_BLK + v), by_head(BB[d])).then_inc(sc_done[d], 1)

            def new_state_b(d, n):
                dve.wait_ge(sub_full[d], n + 1)
                for p in range(2):
                    for h in range(2):
                        r = slice(64 * h, 64 * h + 64)
                        ins = dve.scalar_tensor_tensor(out=state_b[d][r, p, :], in0=state_b[d][r, p, :], scalar=ex[d][r, p, 0, last[d]:last[d] + 1],
                                                       in1=BB[d][r, p * 256 + h * P:p * 256 + (h + 1) * P], op0=ALU.mult, op1=ALU.add)
                ins.then_inc(bs_done[d], 1)

            def residual(d, n, u):
                dve.wait_ge(ks_full[d], n + 1)
                dve.wait_ge(esm_done[d], n + 1)
                for h in range(HA):
                    ins = dve.scalar_tensor_tensor(out=resid[d][:, h, :], in0=BX[d][:, h * P:(h + 1) * P], scalar=esm[d][:, h:h + 1],
                                                   in1=rin[d][u][:, R_V + h * P:R_V + (h + 1) * P], op0=ALU.mult, op1=ALU.subtract)
                ins.then_inc(r_done[d], 1)

            def new_v(d, n, u):
                dve.wait_ge(z_full[d], n + 1)
                dve.tensor_tensor(v_new[d][:, :, :], by_head(BT_[d]), lanes(rin[d][u][:, R_NB + 4 * d:R_NB + 4 * d + 4], P), ALU.mult).then_inc(vn_done[d], 1)

            def add_a(d, n):
                dve.wait_ge(oi_full[d], n - 1)
                dve.wait_ge(qs_out[d], n - 1)
                wait(dve, out_st[d], 16 * (n - 2))
                dve.tensor_tensor(outb[d][:, 0:512].rearrange("p (h n) -> p h n", h=HA), by_head(BX[d]), o_inter[d][:, :, :], ALU.add).then_inc(oa_done[d], 1)

            def new_state_a(d, n):
                dve.wait_ge(su_full[d], n + 1)
                for h in range(HA):
                    ins = dve.scalar_tensor_tensor(out=state_a[d][:, h, :], in0=state_a[d][:, h, :], scalar=esm[d][:, 4 + h:5 + h],
                                                   in1=BY[d][:, h * P:(h + 1) * P], op0=ALU.mult, op1=ALU.add)
                ins.then_inc(s_done[d], 1)

            def step(n, u, ctx_step):
                both(sums, n)
                both(system, n, u)
                both(first, n)
                for l in range(NLEV - 1):
                    both(level, n, l)
                    if l == 0:
                        both(decayed_k, n, u)
                    elif l == 1:
                        decayed_q(n, u)
                    if l >= 1:
                        both(mask_scores, n, l - 1)
                both(level, n, NLEV - 1)
                both(residual, n, u)
                both(new_v, n, u)
                if not ctx_step:
                    both(add_a, n)
                both(new_state_b, n)
                both(new_state_a, n)

            for n in range(2):
                step(n, n, True)
            with dve.Fori(1, CHUNKS // 2) as i:
                for u in range(2):
                    step(2 * i + u, u, False)

        @block.gpsimd
        def _(pool):
            pool.memset(ql[0][:, :, :, :, :], 0.0)
            pool.wait_ge(tab_in, 16)

            def mask_decay(d, n):
                pool.wait_ge(dd_done[d], n + 1)
                pool.tensor_tensor(decay[d][:, :, :], decay[d][:, :, :], rows(const(C_NEG, d), HA), ALU.add).then_inc(ddm_done[d], 1)

            def decayed_q(n, u):
                pool.wait_ge(ex_done[0], 3 * n + 3)
                wait(pool, sub_full[0], n)
                scale_q(pool, 0, u).then_inc(ql_done[0], 1)

            def decayed_v(d, n):
                pool.wait_ge(vn_done[d], n + 1)
                pool.wait_ge(esm_done[d], n + 1)
                pool.tensor_tensor(v_dec[d][:, :, :], v_new[d][:, :, :], lanes(esm[d][:, 8:12], P), ALU.mult).then_inc(vd_done[d], 1)

            def mod_piece(n):
                pool.wait_ge(ql_done[0], n + 1)
                pool.wait_ge(wmod_in, 16 * (n - 1))
                pool.tensor_tensor(wst[:, :, :], wst[:, :, :], lanes(silu_c[:, 0, :], MODC), ALU.mult).then_inc(mod_step, 1)
                pool.wait_ge(mod_step, MOD_STEPS * (n - 2) + 1)
                pool.tensor_tensor(wst[:, 0:4, :], wst[:, 0:4, :], wst[:, 4:8, :], ALU.add).then_inc(mod_step, 1)
                pool.wait_ge(mod_step, MOD_STEPS * (n - 2) + 2)
                pool.tensor_tensor(wst[:, 0:2, :], wst[:, 0:2, :], wst[:, 2:4, :], ALU.add).then_inc(mod_step, 1)
                pool.wait_ge(mod_step, MOD_STEPS * (n - 2) + 3)
                wait(pool, mod_st, 16 * (n - 2))
                pool.tensor_tensor(mod_acc[:, :], wst[:, 0, :], wst[:, 1, :], ALU.add).then_inc(mod_step, 1)

            def step(n, u, ctx_step):
                both(mask_decay, n)
                decayed_q(n, u)
                if not ctx_step:
                    mod_piece(n)
                both(decayed_v, n)

            for n in range(2):
                step(n, n, True)
            with pool.Fori(1, CHUNKS // 2) as i:
                for u in range(2):
                    step(2 * i + u, u, False)


TILES = 4
NB = SEQ // P // TILES
G_PAIRS = FC // 2
GROUPS = [(0, 12), (12, FC)]
DOWN = [(g, half, f) for g, (f0, f1) in enumerate(GROUPS) for half in range(2) for f in range(f0, f1)]
DOWN_INCS = sum(2 * (f1 - f0 - 1) for f0, f1 in GROUPS)
OB = 8 + 8 * len(GROUPS)
DB = 8 * len(GROUPS)


def stage_ffn(nc, t, rec, mixed, out, col, mod_sums):
    with ExitStack() as ctx:
        sb = lambda name, shape, dt=F32: ctx.enter_context(nc.sbuf_tensor(name, shape, dt))
        sem, clear = semaphores(nc)
        ctx.callback(clear)

        def halves(name, shape):
            offset = (nc.sbuf_base + 31) // 32 * 32
            return sb(name, shape), nc.alloc_sbuf_tensor_at(f"{name}_r", shape, F32R, offset=offset)

        tab = sb("tab4", [P, 2, P])
        ident, ones = tab[:, 0, :], tab[:, 1, :]
        g1b, g2b, fin = sb("g1b", [P, D]), sb("g2b", [P, D]), sb("fin", [P, D])
        gain2, shift2 = sb("gain2", [P, KD]), sb("shift2", [P, KD])
        head_gain = sb("head_gain", [P, 2])
        eps = sb("eps4", [P, 1])
        ld = sb("ld", [P, 3, D])
        gated = sb("gated", [P, TILES, D])
        x1 = sb("x1", [P, TILES, D])
        (hT_lo, hT_lo_r), hT_hi = halves("hT_lo", [P, KD, TILES * P]), sb("hT_hi", [P, KD, TILES * P], F32R)
        NG = GROUPS[0][1]
        (hid_lo, hid_lo_r), hid_hi = halves("hid_lo", [P, NG, TILES * P]), sb("hid_hi", [P, NG, TILES * P], F32R)
        mixT = hid_lo[:, 0:4, :].rearrange("p (u a) (b n) -> p u (a b) n", u=2, n=P)
        gu, gu_r = zip(*[halves(f"gu{i}", [P, 2, KD, 256]) for i in range(2)])
        gu_hi, gu_hi_r = halves("gu_hi", [P, 2, 2, KD, P])
        wout = [gu_hi[:, :, :, :, :].rearrange("p u a k n -> p (u a k n)").rearrange("p (k n) -> p k n", k=KD),
                gu[1][:, :, :, :].rearrange("p a k n -> p (a k n)").rearrange("p (k n) -> p k n", k=KD)]
        (wd, wd_lo_r), wd_hi = halves("wd", [P, 4, 512]), sb("wd_hi", [P, 2, 512], F32R)
        sg = sb("sg", [P, 2, 512])
        scratch = sg[:, :, :].rearrange("p a b -> p (a b)")
        tmp = sb("tmp", [P, 2, 512])
        ss8, r8 = sb("ss8", [P, 8]), sb("r8", [P, 8])
        ss, rstd = sb("ss4", [P, TILES]), sb("rstd4", [P, TILES])
        GA = [ctx.enter_context(nc.psum_tensor(f"ga{i}", [P, 512], F32)) for i in range(4)]
        DN = [ctx.enter_context(nc.psum_tensor(f"dn{i}", [P, 512], F32)) for i in range(4)]

        sums = gu[0][:, :, :, :].rearrange("p a k n -> p (a k n)").rearrange("p (g n) -> p g n", n=512)
        sums_by_piece = gu[0][:, :, :, :].rearrange("p a k n -> p (a k n)").rearrange("p (g n) -> p g n", n=MODC)
        sums_in = sem("sums_in")
        const_in, wout_in, eps_done = sem("const_in"), sem("wout_in"), sem("eps_done")
        mod_full, mod_done, rows_done = sem("mod_full4"), sem("mod_done4"), sem("rows_done")
        ld_in, o_sum, o_sq, ss8_done, r8_ln, r8_done, z_silu, o_norm, gated_done = (
            sem("ld_in"), sem("o_sum"), sem("o_sq"), sem("ss8_done"), sem("r8_ln"), sem("r8_done"), sem("z_silu"), sem("o_norm"), sem("gated_done"))
        x_in, m_full, m_out, o_full, o_read, add_done = sem("x_in4"), sem("m_full"), sem("m_out"), sem("o_full"), sem("o_read"), sem("add_done")
        ss_done, st_ln, rstd_done, xn_done, h_full, h_act, h_dve = (
            sem("ss_done4"), sem("st_ln"), sem("rstd_done4"), sem("xn_done"), sem("h_full"), sem("h_act"), sem("h_dve"))
        gu_in = [sem(f"gu_in{i}") for i in range(2)]
        wd_in = [sem(f"wd_in{i}") for i in range(4)]
        gate_full, up_full, sg_done, hid_done, wd_used, dn_full = sem("gate_full"), sem("up_full"), sem("sg_done"), sem("hid_done"), sem("wd_used"), sem("dn_full")
        raw_done, hid_split, gu_split, gu_done = sem("raw_done"), sem("hid_split"), sem("gu_split"), sem("gu_done")
        h_split, h_done, wd_split, wd_done = sem("h_split"), sem("h_done"), sem("wd_split"), sem("wd_done")
        y_norm, y_done, y_out = sem("y_norm"), sem("y_done"), sem("y_out")
        block = ctx.enter_context(nc.Block())

        x_v = t["x"].rearrange("o (b t p) d -> (o b) p t d", t=TILES, p=P)
        out_v = out.rearrange("o (b t p) d -> (o b) p t d", t=TILES, p=P)
        wg_v = t["w_gate"].rearrange("o (k p) n -> (o p) k n", p=P)
        wu_v = t["w_up"].rearrange("o (k p) n -> (o p) k n", p=P)
        wd_v = t["w_down"].rearrange("o (f p) n -> (o p) f n", p=P)
        wout_v = t["w_out"].rearrange("o (k p) n -> (o p) k n", p=P)
        GATE_AT = {3: 0, 8: 1, 13: 2, 18: 3}

        def gu_piece(f):
            raw, lo = (x[f // 2 % 2][:, :, :, (f % 2) * P:(f % 2 + 1) * P] for x in (gu, gu_r))
            return raw, lo, gu_hi_r[:, f % 2, :, :, :]

        def down_pieces(g):
            return [j for j, piece in enumerate(DOWN) if piece[0] == g]

        def wd_gone(b, j):
            g, half, f = DOWN[j]
            f0, f1 = GROUPS[g]
            if f < f1 - 1:
                before = sum(1 for g_, _, f_ in DOWN[:j] if f_ < GROUPS[g_][1] - 1)
                return wd_used, DOWN_INCS * b + before + 1
            return dn_full, DB * b + 8 * g + 4 * half + 4

        @block.sync
        def _(sp):
            sp.dma_start(tab[:, :, :], t["table"][:, 0:2 * P].rearrange("p (a b) -> p a b", a=2)).then_inc(const_in, 16)
            for n, name in enumerate(("gdn_norm", "gla_norm")):
                sp.dma_start(head_gain[:, n:n + 1], t[name].rearrange("o p -> p o")).then_inc(const_in, 16)
            sp.dma_start(fin[:, :], t["final_norm"].unsqueeze(0).broadcast_to([P, D])).then_inc(const_in, 16)
            for g, c in ((g1b, 2 * D), (g2b, 5 * D)):
                sp.dma_start(g[:, :], t["b_mod"][:, c:c + D].broadcast_to([P, D])).then_inc(const_in, 16)

            def held(*pairs):
                values = [v if isinstance(v, int) else sp.to_reg(v) for v in pairs[1::2]]
                sp.wait_ge(const_in, 96)
                for sem_, v in zip(pairs[::2], values):
                    wait(sp, sem_, v)

            def load_tile(T):
                held(gated_done, T)
                for d in range(2):
                    sp.dma_start(ld[:, d, :], mixed[d, T]).then_inc(ld_in, 16)
                sp.dma_start(ld[:, 2, :], rec[T + CHUNKS_CTX, :, R_Z:REC]).then_inc(ld_in, 16)

            load_tile(0)
            sp.dma_start(sums_by_piece, mod_sums.rearrange("g p n -> p g n")).then_inc(sums_in, 16)
            load_tile(1)
            for half in range(2):
                sp.dma_start(wout[half], wout_v[:, :, 512 * half:512 * half + 512]).then_inc(wout_in, 16)
            sp.wait_ge(wout_in, 32)
            sp.dma_start(x1[:, :, :], x_v[0]).then_inc(x_in, 16)
            for T in range(2, TILES):
                load_tile(T)

            def load_gu(b, q):
                held(up_full, FC * b + max(2 * q - 2, 0))
                for m, w in enumerate((wg_v, wu_v)):
                    sp.dma_start(gu[q % 2][:, m, :, :], w[:, :, 256 * q:256 * q + 256]).then_inc(gu_in[q % 2], 16)

            def load_wd(b, j):
                _, half, f = DOWN[j]
                if j >= 4:
                    held(*wd_gone(b, j - 4))
                else:
                    held(wd_used, DOWN_INCS * b, dn_full, DB * b)
                sp.dma_start(wd[:, j % 4, :], wd_v[:, f, 512 * half:512 * half + 512]).then_inc(wd_in[j % 4], 16)

            def main(b, last):
                held(o_full, 8 * (b + 1))
                load_gu(b, 1)

                def next_tile(i):
                    if not last:
                        load_tile(TILES * (b + 1) + i)

                n0 = 2 * NG
                next_tile(0)
                for q in range(2, 5):
                    load_gu(b, q)
                next_tile(1)
                load_gu(b, 5)
                for j in range(4):
                    load_wd(b, j)
                load_gu(b, 6)
                next_tile(2)
                load_gu(b, 7)
                for j in range(4, n0):
                    load_wd(b, j)
                load_gu(b, 8)
                next_tile(3)
                load_gu(b, 9)
                for j in range(n0, n0 + 4):
                    load_wd(b, j)
                load_gu(b, 10)
                if not last:
                    held(up_full, FC * b + 20)
                    sp.dma_start(wout[1], wout_v[:, :, 512:D]).then_inc(wout_in, 16)
                for j in range(n0 + 4, len(DOWN)):
                    load_wd(b, j)
                    if not last and j % 2 == 1 and j < n0 + 12:
                        q = (j - n0 - 5) // 2
                        held(up_full, FC * (b + 1))
                        sp.dma_start(wout[0][:, 2 * q:2 * q + 2, :], wout_v[:, 2 * q:2 * q + 2, 0:512]).then_inc(wout_in, 16)
                if not last:
                    load_gu(b + 1, 0)
                for i in range(TILES):
                    held(y_done, TILES * b + i + 1)
                    sp.dma_start(out_v[b, :, i, :], x1[:, i, :]).then_inc(y_out, 16)
                if not last:
                    held(y_out, 16 * TILES * (b + 1))
                    sp.dma_start(x1[:, :, :], x_v[b + 1]).then_inc(x_in, 16)

            sp.wait_ge(rows_done, 4)
            sp.wait_ge(mod_done, 2)
            load_gu(0, 0)
            with sp.Fori(0, NB - 1) as b:
                main(b, False)
            main(NB - 1, True)
            sp.wait_ge(y_out, 16 * TILES * NB)

        @block.tensor
        def _(pe):
            pe.wait_ge(const_in, 96)
            pe.wait_ge(sums_in, 16)
            for c in range(2 * KD):
                mm = pe.matmul(DN[0][:, c:c + 1], sums[:, 2 + c // 4, (c % 4) * P:(c % 4 + 1) * P], ones[:, 0:1], start=True, stop=True)
            mm.then_inc(mod_full, 1)
            for n, g in enumerate((0, 1, 6, 7)):
                pe.matmul(GA[n][:, :], ones, sums[:, g, :], start=True, stop=True).then_inc(mod_full, 1)
            pe.wait_ge(mod_done, 3)
            pe.wait_ge(rows_done, 4)

            def turn_mixed(b, i):
                T = TILES * b + i
                pe.wait_ge(gated_done, T + 1)
                wait(pe, m_out, T)
                if i == 0:
                    wait(pe, raw_done, FC * b)
                for k in range(KD):
                    mm = pe.transpose(GA[k // 4][:, (k % 4) * P:(k % 4 + 1) * P], gated[:, i, k * P:(k + 1) * P], ident[:, :])
                mm.then_inc(m_full, 1)

            def project(b, i):
                T = TILES * b + i
                pe.wait_ge(m_out, T + 1)
                if i == 0:
                    pe.wait_ge(wout_in, 32 + 80 * b)
                for half in range(2):
                    wait(pe, o_read, OB * b + 2 * i + half - 3 if i >= 2 else OB * b)
                    for k in range(KD):
                        mm = pe.matmul(DN[2 * (i % 2) + half][:, :], mixT[:, i % 2, k, :], wout[half][:, k, :],
                                       start=k == 0, stop=k == KD - 1)
                    mm.then_inc(o_full, 1)

            def turn_norm(b, i):
                T = TILES * b + i
                pe.wait_ge(xn_done, T + 1)
                wait(pe, h_act, T)
                wait(pe, h_dve, T)
                for k in range(KD):
                    mm = pe.transpose(GA[2 + k // 4][:, (k % 4) * P:(k % 4 + 1) * P], gated[:, i, k * P:(k + 1) * P], ident[:, :])
                mm.then_inc(h_full, 1)

            def main(b, last):
                for s in range(TILES + 2):
                    if s < TILES:
                        turn_mixed(b, s)
                    if 1 <= s <= TILES:
                        project(b, s - 1)
                    if s >= 2:
                        turn_norm(b, s - 2)
                pe.wait_ge(h_done, TILES * (b + 1))
                for g, (f0, f1) in enumerate(GROUPS):
                    for f in range(f0, f1):
                        pe.wait_ge(gu_done, FC * b + f + 1)
                        if f >= 2:
                            pe.wait_ge(raw_done, FC * b + f - 1)
                        _, lo, hi = gu_piece(f)
                        for m in range(2):
                            for k in range(KD):
                                terms = (hi, hT_hi), (hi, hT_lo_r), (lo, hT_hi)
                                for n, (w, h) in enumerate(terms):
                                    mm = pe.matmul(GA[2 * (f % 2) + m][:, :], w[:, m, k, :], h[:, k, :],
                                                   start=k == 0 and n == 0, stop=k == KD - 1 and n == 2)
                            mm.then_inc(up_full if m else gate_full, 1)
                    for half in range(2):
                        for f in range(f0, f1):
                            j = DOWN.index((g, half, f))
                            pe.wait_ge(wd_done, len(DOWN) * b + j + 1)
                            pe.wait_ge(hid_done, FC * b + f + 1)
                            for i in range(TILES):
                                if f == f0:
                                    n = 8 + 8 * g + 4 * half
                                    pe.wait_ge(o_read, OB * b + (n if n == 8 else n - 4 + i + 1))
                                at = slice(i * P, (i + 1) * P)
                                terms = (hid_hi, wd_hi[:, j % 2, :]), (hid_hi, wd_lo_r[:, j % 4, :]), (hid_lo_r, wd_hi[:, j % 2, :])
                                for n, (h, w) in enumerate(terms):
                                    mm = pe.matmul(DN[i][:, :], h[:, f - f0, at], w, start=f == f0 and n == 0, stop=f == f1 - 1 and n == 2)
                                if f == f1 - 1:
                                    mm.then_inc(dn_full, 1)
                            if f < f1 - 1:
                                mm.then_inc(wd_used, 1)

            with pe.Fori(0, NB - 1) as b:
                main(b, False)
            main(NB - 1, True)

        @block.scalar
        def _(act):
            def table_ln_exp():
                act.preload_act_table_set("natural_log_exp_and_others")

            def gate(T):
                act.wait_ge(ld_in, 48 * (T + 1))
                act.activation(ld[:, 2, :], ld[:, 2, :], ACT.Silu).then_inc(z_silu, 1)
                table_ln_exp()
                act.wait_ge(ss8_done, T + 1)
                wait(act, o_norm, T)
                act.activation(r8[:, :], ss8[:, :], ACT.Ln, scale=1.0 / P, bias=eps[:, :]).then_inc(r8_ln, 1)
                act.wait_ge(r8_ln, T + 1)
                act.activation(r8[:, :], r8[:, :], ACT.Exp, scale=-0.5).then_inc(r8_done, 1)

            def stats(i, n):
                wait(act, ss_done, n)
                act.activation(scratch, x1[:, i, :], ACT.Square, accum_out=ss[:, i:i + 1]).then_inc(ss_done, 1)
                act.wait_ge(ss_done, n + 1)
                act.activation(rstd[:, i:i + 1], ss[:, i:i + 1], ACT.Ln, scale=1.0 / D, bias=eps[:, :]).then_inc(st_ln, 1)
                act.wait_ge(st_ln, n + 1)
                act.activation(rstd[:, i:i + 1], rstd[:, i:i + 1], ACT.Exp, scale=-0.5).then_inc(rstd_done, 1)

            act.wait_ge(eps_done, 1)
            gate(0)
            act.wait_ge(const_in, 96)
            gate(1)

            def mixed_out(b, i):
                T = TILES * b + i
                act.wait_ge(m_full, T + 1)
                wait(act, o_full, 8 * b + 2 * (i - 1) if i >= 2 else 8 * b)
                for g in range(2):
                    ins = act.activation(mixT[:, i % 2, 4 * g:4 * g + 4, :], GA[g][:, :].rearrange("p (a b) -> p a b", b=P), ACT.Copy,
                                         scale=head_gain[:, g:g + 1])
                ins.then_inc(m_out, 1)

            def norm_out(b, i):
                T = TILES * b + i
                act.wait_ge(h_full, T + 1)
                for k in range(4):
                    ins = act.activation(hT_lo[:, k, i * P:(i + 1) * P], GA[2][:, k * P:(k + 1) * P], ACT.Identity,
                                         scale=gain2[:, k:k + 1], bias=shift2[:, k:k + 1])
                ins.then_inc(h_act, 1)
                act.wait_ge(h_dve, T + 1)
                act.wait_ge(h_act, T + 1)
                at = slice(i * P, (i + 1) * P)
                act.activation(hT_hi[:, :, at], hT_lo[:, :, at], ACT.Copy).then_inc(h_split, 1)

            def split_gu(b, f):
                q = f // 2
                n = (G_PAIRS + 1) // 2 if q % 2 == 0 else G_PAIRS // 2
                act.wait_ge(gu_in[q % 2], 32 * (n * b + q // 2 + 1))
                if f >= 2:
                    act.wait_ge(up_full, FC * b + f - 1)
                else:
                    act.wait_ge(o_full, 8 * (b + 1))
                raw, _, hi = gu_piece(f)
                for m in range(2):
                    ins = act.activation(hi[:, m, :, :], raw[:, m, :, :], ACT.Copy)
                ins.then_inc(gu_split, 1)

            def split_hid(b, f, f0):
                act.wait_ge(raw_done, FC * b + f + 1)
                act.activation(hid_hi[:, f - f0, :], hid_lo[:, f - f0, :], ACT.Copy).then_inc(hid_split, 1)

            def split_wd(b, j):
                act.wait_ge(wd_in[j % 4], 16 * (len(DOWN) // 4 * b + j // 4 + 1))
                if j >= 2:
                    act.wait_ge(*wd_gone(b, j - 2))
                act.activation(wd_hi[:, j % 2, :], wd[:, j % 4, :], ACT.Copy).then_inc(wd_split, 1)

            def main(b, last, first=False):
                for s in range(TILES + 2):
                    if s < TILES:
                        if s > 0 or first:
                            mixed_out(b, s)
                        if first and s in (1, 2):
                            gate(s + 1)
                    if s >= 2:
                        norm_out(b, s - 2)
                    if 1 <= s <= TILES:
                        act.wait_ge(add_done, OB * b + 2 * s)
                        stats(s - 1, 8 * b + s - 1)
                split_gu(b, 0)
                for g, (f0, f1) in enumerate(GROUPS):
                    for f in range(f0, f1):
                        if f + 1 < FC:
                            split_gu(b, f + 1)
                        if f > f0:
                            split_hid(b, f - 1, f0)
                        if f == f1 - 1:
                            for j in down_pieces(g)[:2]:
                                split_wd(b, j)
                        act.wait_ge(gate_full, FC * b + f + 1)
                        if f >= 2:
                            act.wait_ge(raw_done, FC * b + f - 1)
                        elif f == 0:
                            act.wait_ge(ss_done, 8 * b + 4)
                        act.activation(sg[:, f % 2, :], GA[2 * (f % 2)][:, :], ACT.Silu).then_inc(sg_done, 1)
                        if f in GATE_AT and not last:
                            gate(TILES * (b + 1) + GATE_AT[f])
                    split_hid(b, f1 - 1, f0)
                    for j in down_pieces(g)[2:]:
                        split_wd(b, j)
                table_ln_exp()
                if not last:
                    act.wait_ge(dn_full, DB * (b + 1))
                    mixed_out(b + 1, 0)
                act.wait_ge(raw_done, FC * (b + 1))
                for i in range(TILES):
                    act.wait_ge(add_done, OB * (b + 1) - TILES + i + 1)
                    stats(i, 8 * b + 4 + i)

            main(0, False, True)
            with act.Fori(1, NB - 1) as b:
                main(b, False)
            main(NB - 1, True)

        @block.vector
        def _(dve):
            dve.memset(eps[:, :], EPS).then_inc(eps_done, 1)

            def gate(T, i):
                dve.wait_ge(o_sq, T + 1)
                wait(dve, r8_done, T)
                dve.tensor_reduce(ss8[:, :], ld[:, 1, :].rearrange("p (h n) -> p h n", n=P), AX.X, ALU.add).then_inc(ss8_done, 1)
                dve.wait_ge(r8_done, T + 1)
                o = ld[:, 0, :].rearrange("p (h n) -> p h n", n=P)
                dve.tensor_tensor(o, o, lanes(r8[:, :], P), ALU.mult).then_inc(o_norm, 1)
                dve.wait_ge(o_norm, T + 1)
                dve.wait_ge(z_silu, T + 1)
                dve.tensor_tensor(gated[:, i, :], ld[:, 0, :], ld[:, 2, :], ALU.mult).then_inc(gated_done, 1)

            gate(0, 0)
            dve.wait_ge(const_in, 96)
            dve.wait_ge(mod_full, 1)
            dve.tensor_tensor(shift2[:, :], DN[0][:, 0:KD], col[:, 3 * KD:4 * KD], ALU.add).then_inc(mod_done, 1)
            dve.tensor_tensor(gain2[:, :], DN[0][:, KD:2 * KD], col[:, 4 * KD:5 * KD], ALU.add).then_inc(mod_done, 1)
            dve.wait_ge(mod_done, 2)
            dve.scalar_tensor_tensor(out=gain2[:, :], in0=gain2[:, :], scalar=1.0, in1=col[:, 56:64], op0=ALU.add, op1=ALU.mult).then_inc(mod_done, 1)
            for n, (g, half) in enumerate(((g1b, 0), (g1b, 1), (g2b, 0), (g2b, 1))):
                dve.wait_ge(mod_full, n + 2)
                r = g[:, half * 512:half * 512 + 512]
                dve.tensor_tensor(r, GA[n][:, :], r, ALU.add).then_inc(rows_done, 1)
            dve.wait_ge(rows_done, 4)
            gate(1, 1)

            def scaled(b, n, bank, g, half):
                wait(dve, add_done, OB * b + max(n - 1, 0))
                dve.tensor_tensor(tmp[:, n % 2, :], bank[:, :], g[:, half * 512:half * 512 + 512], ALU.mult).then_inc(o_read, 1)

            def projected(b, i):
                for half in range(2):
                    dve.wait_ge(o_full, 8 * b + 2 * i + half + 1)
                    scaled(b, 2 * i + half, DN[2 * (i % 2) + half], g1b, half)

            def normalized(b, i):
                dve.wait_ge(rstd_done, 8 * b + i + 1)
                dve.tensor_scalar(gated[:, i, :], x1[:, i, :], rstd[:, i:i + 1], None, ALU.mult).then_inc(xn_done, 1)

            def norm_out(b, i):
                dve.wait_ge(h_full, TILES * b + i + 1)
                for k in range(4, KD):
                    ins = dve.tensor_scalar(hT_lo[:, k, i * P:(i + 1) * P], GA[3][:, (k - 4) * P:(k - 3) * P], gain2[:, k:k + 1],
                                            shift2[:, k:k + 1], ALU.mult, ALU.add)
                ins.then_inc(h_dve, 1)
                dve.wait_ge(h_split, TILES * b + i + 1)
                at = slice(i * P, (i + 1) * P)
                minus_hi(hT_lo_r[:, :, at], hT_lo[:, :, at], hT_hi[:, :, at]).then_inc(h_done, 1)

            def minus_hi(lo, x, hi):
                return dve.tensor_tensor(lo, x, hi, ALU.subtract)

            def rest_gu(b, f):
                dve.wait_ge(gu_split, FC * b + f + 1)
                raw, lo, hi = gu_piece(f)
                for m in range(2):
                    ins = minus_hi(lo[:, m, :, :], raw[:, m, :, :], hi[:, m, :, :])
                ins.then_inc(gu_done, 1)

            def hidden(b, f, f0):
                dve.wait_ge(up_full, FC * b + f + 1)
                dve.wait_ge(sg_done, FC * b + f + 1)
                dve.tensor_tensor(hid_lo[:, f - f0, :], GA[2 * (f % 2) + 1][:, :], sg[:, f % 2, :], ALU.mult).then_inc(raw_done, 1)

            def rest_hid(b, f, f0):
                dve.wait_ge(hid_split, FC * b + f + 1)
                minus_hi(hid_lo_r[:, f - f0, :], hid_lo[:, f - f0, :], hid_hi[:, f - f0, :]).then_inc(hid_done, 1)

            def rest_wd(b, j):
                dve.wait_ge(wd_split, len(DOWN) * b + j + 1)
                minus_hi(wd_lo_r[:, j % 4, :], wd[:, j % 4, :], wd_hi[:, j % 2, :]).then_inc(wd_done, 1)

            def out_banks(b, g, half):
                for i in range(TILES):
                    dve.wait_ge(dn_full, DB * b + 8 * g + 4 * half + i + 1)
                    scaled(b, 8 + 8 * g + 4 * half + i, DN[i], g2b, half)

            def main(b, last, first=False):
                for i in range(TILES):
                    if first and i < 2:
                        gate(i + 2, i + 2)
                    projected(b, i)
                    if i >= 1:
                        norm_out(b, i - 1)
                    normalized(b, i)
                norm_out(b, TILES - 1)
                rest_gu(b, 0)
                for g, (f0, f1) in enumerate(GROUPS):
                    for f in range(f0, f1):
                        if f > f0:
                            hidden(b, f - 1, f0)
                        if f + 1 < FC:
                            rest_gu(b, f + 1)
                        if f > f0:
                            rest_hid(b, f - 1, f0)
                        if f == f1 - 1:
                            for j in down_pieces(g)[:2]:
                                rest_wd(b, j)
                        if f in GATE_AT and not last:
                            gate(TILES * (b + 1) + GATE_AT[f], GATE_AT[f])
                    hidden(b, f1 - 1, f0)
                    rest_hid(b, f1 - 1, f0)
                    for j in down_pieces(g)[2:]:
                        rest_wd(b, j)
                        if DOWN[j] == (g, 1, f0):
                            out_banks(b, g, 0)
                    out_banks(b, g, 1)
                for i in range(TILES):
                    dve.wait_ge(rstd_done, 8 * b + 4 + i + 1)
                    dve.tensor_scalar(x1[:, i, :], x1[:, i, :], rstd[:, i:i + 1], None, ALU.mult).then_inc(y_norm, 1)

            main(0, False, True)
            with dve.Fori(1, NB - 1) as b:
                main(b, False)
            main(NB - 1, True)

        @block.gpsimd
        def _(pool):
            def gate(T):
                pool.wait_ge(ld_in, 48 * (T + 1))
                pool.tensor_tensor(ld[:, 0, :], ld[:, 0, :], ld[:, 1, :], ALU.add).then_inc(o_sum, 1)
                pool.wait_ge(o_sum, T + 1)
                pool.tensor_tensor(ld[:, 1, :], ld[:, 0, :], ld[:, 0, :], ALU.mult).then_inc(o_sq, 1)

            gate(0)
            gate(1)

            def add(b, n, i, half):
                pool.wait_ge(o_read, OB * b + n + 1)
                x = x1[:, i, half * 512:half * 512 + 512]
                pool.tensor_tensor(x, x, tmp[:, n % 2, :], ALU.add).then_inc(add_done, 1)

            def main(b, last, first=False):
                for i in range(TILES):
                    if first and i < 2:
                        gate(i + 2)
                    if i == 0:
                        pool.wait_ge(x_in, 16 * (b + 1))
                    for half in range(2):
                        add(b, 2 * i + half, i, half)
                for n in range(8, OB):
                    i, half = n % TILES, n // TILES % 2
                    if n % 8 == 0 and not last:
                        for f in range(*GROUPS[n // 8 - 1]):
                            if f in GATE_AT:
                                gate(TILES * (b + 1) + GATE_AT[f])
                    if n < 8 + TILES:
                        pool.wait_ge(xn_done, TILES * b + i + 1)
                    add(b, n, i, half)
                for i in range(TILES):
                    pool.wait_ge(y_norm, TILES * b + i + 1)
                    pool.tensor_tensor(x1[:, i, :], x1[:, i, :], fin[:, :], ALU.mult).then_inc(y_done, 1)

            main(0, False, True)
            with pool.Fori(1, NB - 1) as b:
                main(b, False)
            main(NB - 1, True)


def layer(nc, t, out):
    rec = nc.dram_tensor("records", [CHUNKS, P, REC], F32, kind="Internal").ap()
    mixed = nc.dram_tensor("mixed", [2, CHUNKS - CHUNKS_CTX, P, 1024], F32, kind="Internal").ap()
    mod_sums = nc.dram_tensor("mod_sums", [4 * D // MODC, P, MODC], F32, kind="Internal").ap()
    with ExitStack() as ctx:
        col = ctx.enter_context(nc.sbuf_tensor("col", [P, 116], F32))
        silu_c = ctx.enter_context(nc.sbuf_tensor("silu_c", [P, 2, KD], F32))
        stage_project(nc, t, rec, col, silu_c)
        stage_mixers(nc, t, rec, mixed, silu_c, mod_sums)
        stage_ffn(nc, t, rec, mixed, out, col, mod_sums)


INS = ["x", "c", "ctx", "c_ctx", "w_mod", "b_mod", "attn_norm", "w_in", "conv_w", "a_log", "dt_bias", "gdn_norm",
       "gla_w2", "gla_b", "gla_norm", "w_out", "ffn_norm", "w_gate", "w_up", "w_down", "final_norm"]


def kernel(**inputs):
    import numpy as _np
    import concourse.bacc as _bacc
    from concourse import mybir as _mybir
    from concourse.bass_utils import run_bass_kernel_spmd as _run

    nc = _bacc.Bacc("TRN2", target_bir_lowering=False, num_devices=1)
    arrays, args = {}, {}
    table, masks = tables()
    for name in [*INS, "table", "masks"]:
        a = _np.ascontiguousarray({"table": table, "masks": masks}[name] if name in ("table", "masks") else inputs[name])
        arrays[f"in_{name}_dram"] = a
        args[name] = nc.dram_tensor(f"in_{name}_dram", a.shape, _mybir.dt.from_np(a.dtype), kind="ExternalInput").ap()
    out = nc.dram_tensor("out_0_dram", (1, SEQ, D), F32, kind="ExternalOutput").ap()
    layer(nc, args, out)
    r = _run(nc, [arrays], core_ids=[0])
    return r.results[0]["out_0_dram"]
```
